# Optimizing a Trainium2 kernel written in Bass

```python
import math
import jax, jax.numpy as jnp
from jax import lax
import numpy as np

D_MODEL = 1024
BATCH = 1
SEQ = 512
DEPTH = 2

N_META = 16
N_EVEN = (DEPTH + 1) // 2
N_ODD = DEPTH // 2

S5_WIDTH = D_MODEL // 2
S5_GROUP = 16
S5_GROUPS = S5_WIDTH // S5_GROUP
S5_STATE = 64
S5_DT_MIN = 0.001
S5_DT_MAX = 0.1

SB_HEAD_DIM = 64
SB_WIDTH = D_MODEL // 2
SB_HEADS = SB_WIDTH // SB_HEAD_DIM
SB_BLOCK = 128

HG_WIDTH = D_MODEL
HG_DK = 128
HG_HEADS = HG_WIDTH // HG_DK
HG_DV = HG_WIDTH // HG_HEADS
HG_CHUNK = 64

D_FF = 4 * D_MODEL
IN_AB = S5_WIDTH + 3 * SB_WIDTH
IN_C = 4 * HG_WIDTH

ALPHA = (2.0 * DEPTH) ** 0.25
BETA = (8.0 * DEPTH) ** -0.25
LN_EPS = 1e-5
RMS_EPS = 1e-6

kernel_name = 'hybrid_s5_stickbreak_hgrn2_deepnorm_meta'

def layer_norm(x, g, b):
    xf = x.astype(jnp.float32)
    mu = jnp.mean(xf, axis=-1, keepdims=True)
    var = jnp.mean(jnp.square(xf - mu), axis=-1, keepdims=True)
    return (xf - mu) * lax.rsqrt(var + LN_EPS) * g + b

def s5_mixer(u, lam_re, lam_im, log_dt, b_re, b_im, c_re, c_im, d, w_glu, b_glu):
    bn, seq_len, _ = u.shape
    f32 = jnp.float32
    uf = u.astype(f32).reshape(bn, seq_len, S5_GROUPS, S5_GROUP)
    lam = lax.complex(lam_re.astype(f32), lam_im.astype(f32))
    dt = jnp.exp(log_dt.astype(f32))[:, None]
    lam_bar = jnp.exp(lam * dt)
    b_mat = lax.complex(b_re.astype(f32), b_im.astype(f32))
    b_bar = ((lam_bar - 1.0) / lam)[:, :, None] * b_mat
    bu = jnp.einsum('blgh,gph->blgp', uf.astype(jnp.complex64), b_bar)
    a = jnp.broadcast_to(lam_bar, (1, seq_len) + lam_bar.shape)

    def combine(left, right):
        a_l, s_l = left
        a_r, s_r = right
        return a_r * a_l, a_r * s_l + s_r

    _, states = lax.associative_scan(combine, (a, bu), axis=1)
    c_mat = lax.complex(c_re.astype(f32), c_im.astype(f32))
    y = jnp.real(jnp.einsum('blgp,ghp->blgh', states, c_mat)) + d.astype(f32) * uf
    y = jax.nn.gelu(y.reshape(bn, seq_len, S5_WIDTH))
    return y * jax.nn.sigmoid(y @ w_glu + b_glu)

def _stick_breaking_block(qb, kb, vb, start):
    z = jnp.einsum('bhqd,bhkd->bhqk', qb, kb)
    nq = qb.shape[2]
    nk = kb.shape[2]
    visible = jnp.arange(nk)[None, :] < (start + jnp.arange(nq))[:, None]
    log_keep = jnp.where(visible, jax.nn.log_sigmoid(-z), 0.0)
    later = lax.cumsum(log_keep, axis=3, reverse=True) - log_keep
    w = jnp.where(visible, jnp.exp(jax.nn.log_sigmoid(z) + later), 0.0)
    return jnp.einsum('bhqk,bhkd->bhqd', w, vb)

def stick_breaking_attention(q, k, v):
    bn, seq_len = q.shape[0], q.shape[1]
    f32 = jnp.float32
    q = q.astype(f32).transpose(0, 2, 1, 3) * (SB_HEAD_DIM ** -0.5)
    k = k.astype(f32).transpose(0, 2, 1, 3)
    v = v.astype(f32).transpose(0, 2, 1, 3)
    blocks = [(0, N_META)] + [(N_META + i * SB_BLOCK, SB_BLOCK)
                              for i in range((seq_len - N_META) // SB_BLOCK)]
    outs = [_stick_breaking_block(q[:, :, s:s + n], k[:, :, :s + n], v[:, :, :s + n], s)
            for s, n in blocks]
    o = jnp.concatenate(outs, axis=2)
    return o.transpose(0, 2, 1, 3).reshape(bn, seq_len, SB_HEADS * SB_HEAD_DIM)

def hgrn_lower_bound(gamma, layer):
    p = jax.nn.softmax(gamma.astype(jnp.float32), axis=0)
    return (jnp.cumsum(p, axis=0) - p[0])[layer]

def _to_chunks(t, n_chunks):
    bn, _, nh, dd = t.shape
    return t.reshape(bn, n_chunks, HG_CHUNK, nh, dd).transpose(1, 0, 3, 2, 4)

def hgrn2_mixer(q, f_pre, i_in, g, lb, norm_g):
    bn, seq_len, _ = q.shape
    f32 = jnp.float32
    f = lb + (1.0 - lb) * jax.nn.sigmoid(f_pre.astype(f32))
    log_f = jnp.log(f)
    k = 1.0 - f
    pad = HG_CHUNK - N_META
    n_chunks = (seq_len + pad) // HG_CHUNK

    def heads(t, dd):
        t = t.astype(f32).reshape(bn, seq_len, HG_HEADS, dd)
        return _to_chunks(jnp.pad(t, ((0, 0), (pad, 0), (0, 0), (0, 0))), n_chunks)

    qh, kh, vh, lh = heads(q, HG_DK), heads(k, HG_DK), heads(i_in, HG_DV), heads(log_f, HG_DK)
    causal = jnp.tril(jnp.ones((HG_CHUNK, HG_CHUNK), dtype=bool))

    def step(state, xs):
        qc, kc, vc, lc = xs
        b = jnp.cumsum(lc, axis=2)
        b_last = b[:, :, -1:, :]
        q_dec = qc * jnp.exp(b)
        scores = jnp.einsum('bhtd,bhsd->bhts', q_dec, kc * jnp.exp(-b))
        scores = jnp.where(causal, scores, 0.0)
        o = (jnp.einsum('bhts,bhse->bhte', scores, vc)
             + jnp.einsum('bhtd,bhde->bhte', q_dec, state))
        state = (jnp.exp(b_last[:, :, 0, :])[..., None] * state
                 + jnp.einsum('bhsd,bhse->bhde', kc * jnp.exp(b_last - b), vc))
        return state, o

    s0 = jnp.zeros((bn, HG_HEADS, HG_DK, HG_DV), f32)
    _, o = lax.scan(step, s0, (qh, kh, vh, lh))
    o = o.transpose(1, 0, 3, 2, 4).reshape(bn, seq_len + pad, HG_HEADS, HG_DV)[:, pad:]
    o = o * lax.rsqrt(jnp.mean(jnp.square(o), axis=-1, keepdims=True) + RMS_EPS)
    o = o * norm_g.astype(f32).reshape(HG_HEADS, HG_DV)
    return o.reshape(bn, seq_len, HG_WIDTH) * jax.nn.silu(g.astype(f32))

def setup_inputs(seed: int = 0) -> dict:
    key = jax.random.key(seed)
    ks = jax.random.split(key, 32)
    f32 = jnp.float32
    nrm = lambda k, shape, scale: jax.random.normal(k, shape, f32) * scale
    n_arange = jnp.pi * jnp.arange(S5_STATE, dtype=f32)
    return {
        'x': nrm(ks[0], (BATCH, SEQ, D_MODEL), 1.0),
        'meta': nrm(ks[1], (N_META, D_MODEL), 1.0),
        'w_in_ab': nrm(ks[2], (N_EVEN, D_MODEL, IN_AB), D_MODEL ** -0.5),
        's5_lam_re': -0.5 * jnp.exp(nrm(ks[3], (N_EVEN, S5_GROUPS, S5_STATE), 0.05)),
        's5_lam_im': n_arange + nrm(ks[4], (N_EVEN, S5_GROUPS, S5_STATE), 0.01),
        's5_log_dt': jax.random.uniform(ks[5], (N_EVEN, S5_GROUPS), f32,
                                        minval=math.log(S5_DT_MIN), maxval=math.log(S5_DT_MAX)),
        's5_b_re': nrm(ks[6], (N_EVEN, S5_GROUPS, S5_STATE, S5_GROUP), (2.0 * S5_GROUP) ** -0.5),
        's5_b_im': nrm(ks[7], (N_EVEN, S5_GROUPS, S5_STATE, S5_GROUP), (2.0 * S5_GROUP) ** -0.5),
        's5_c_re': nrm(ks[8], (N_EVEN, S5_GROUPS, S5_GROUP, S5_STATE), S5_STATE ** -0.5),
        's5_c_im': nrm(ks[9], (N_EVEN, S5_GROUPS, S5_GROUP, S5_STATE), S5_STATE ** -0.5),
        's5_d': nrm(ks[10], (N_EVEN, S5_GROUPS, S5_GROUP), 1.0),
        's5_w_glu': nrm(ks[11], (N_EVEN, S5_WIDTH, S5_WIDTH), S5_WIDTH ** -0.5),
        's5_b_glu': nrm(ks[12], (N_EVEN, S5_WIDTH), 0.01),
        'w_out_ab': nrm(ks[13], (N_EVEN, S5_WIDTH + SB_WIDTH, D_MODEL), BETA * (S5_WIDTH + SB_WIDTH) ** -0.5),
        'w_in_c': nrm(ks[14], (N_ODD, D_MODEL, IN_C), D_MODEL ** -0.5),
        'hgrn_gamma': nrm(ks[15], (DEPTH, HG_WIDTH), 0.1),
        'hgrn_norm_g': 1.0 + nrm(ks[16], (N_ODD, HG_WIDTH), 0.01),
        'w_out_c': nrm(ks[17], (N_ODD, HG_WIDTH, D_MODEL), BETA * HG_WIDTH ** -0.5),
        'ln_mix_g': 1.0 + nrm(ks[18], (DEPTH, D_MODEL), 0.01),
        'ln_mix_b': nrm(ks[19], (DEPTH, D_MODEL), 0.01),
        'mlp_w_up': nrm(ks[20], (DEPTH, D_MODEL, D_FF), D_MODEL ** -0.5),
        'mlp_b_up': nrm(ks[21], (DEPTH, D_FF), 0.01),
        'mlp_w_down': nrm(ks[22], (DEPTH, D_FF, D_MODEL), BETA * D_FF ** -0.5),
        'mlp_b_down': nrm(ks[23], (DEPTH, D_MODEL), 0.01),
        'ln_mlp_g': 1.0 + nrm(ks[24], (DEPTH, D_MODEL), 0.01),
        'ln_mlp_b': nrm(ks[25], (DEPTH, D_MODEL), 0.01),
    }

def reference(x, meta, w_in_ab, s5_lam_re, s5_lam_im, s5_log_dt, s5_b_re, s5_b_im, s5_c_re, s5_c_im,
              s5_d, s5_w_glu, s5_b_glu, w_out_ab, w_in_c, hgrn_gamma, hgrn_norm_g, w_out_c,
              ln_mix_g, ln_mix_b, mlp_w_up, mlp_b_up, mlp_w_down, mlp_b_down, ln_mlp_g, ln_mlp_b):
    bn = x.shape[0]
    h = jnp.concatenate([jnp.broadcast_to(meta.astype(x.dtype)[None], (bn, N_META, D_MODEL)), x], axis=1)
    seq_len = h.shape[1]
    for layer in range(DEPTH):
        if layer % 2 == 0:
            e = layer // 2
            proj = h @ w_in_ab[e]
            u = proj[..., :S5_WIDTH]
            qkv = proj[..., S5_WIDTH:].reshape(bn, seq_len, 3, SB_HEADS, SB_HEAD_DIM)
            a_out = s5_mixer(u, s5_lam_re[e], s5_lam_im[e], s5_log_dt[e], s5_b_re[e], s5_b_im[e],
                             s5_c_re[e], s5_c_im[e], s5_d[e], s5_w_glu[e], s5_b_glu[e])
            b_out = stick_breaking_attention(qkv[:, :, 0], qkv[:, :, 1], qkv[:, :, 2])
            mix = jnp.concatenate([a_out, b_out], axis=-1) @ w_out_ab[e]
        else:
            o_idx = layer // 2
            proj = h @ w_in_c[o_idx]
            q, f_pre, i_in, g = jnp.split(proj, 4, axis=-1)
            lb = hgrn_lower_bound(hgrn_gamma, layer)
            mix = hgrn2_mixer(q, f_pre, i_in, g, lb, hgrn_norm_g[o_idx]) @ w_out_c[o_idx]
        h = layer_norm(ALPHA * h + mix, ln_mix_g[layer], ln_mix_b[layer])
        hid = jnp.square(jax.nn.relu(h @ mlp_w_up[layer] + mlp_b_up[layer]))
        h = layer_norm(ALPHA * h + hid @ mlp_w_down[layer] + mlp_b_down[layer],
                       ln_mlp_g[layer], ln_mlp_b[layer])
    return h[:, N_META:, :]


_drawn_inputs = setup_inputs


def setup_inputs(seed=0):
    import zlib

    import numpy as np

    out = dict(_drawn_inputs(seed))
    spreads = {}
    factors = {'meta': 3.853,
     's5_lam_re': 64.0,
     's5_lam_im': 49.28,
     's5_log_dt': 51.136,
     's5_b_re': 64.0,
     's5_b_im': 64.0,
     's5_c_re': 64.0,
     's5_c_im': 64.0,
     's5_b_glu': 59.334,
     'hgrn_gamma': 3.03,
     'hgrn_norm_g': 46.612,
     'ln_mix_g': 3.787,
     'ln_mix_b': 3.706,
     'mlp_b_up': 7.979,
     'mlp_b_down': 22.504,
     'ln_mlp_g': 3.774,
     'ln_mlp_b': 3.601}
    for name, (base, spread) in spreads.items():
        noise = np.random.default_rng([zlib.crc32(name.encode()), seed]).standard_normal(out[name].shape)
        drawn = base * np.exp(spread * noise) if base else spread * noise
        out[name] = __import__('jax').numpy.asarray(drawn.astype(out[name].dtype))
    for name, factor in factors.items():
        out[name] = (out[name] * factor).astype(out[name].dtype)
    return out
```

```python
from contextlib import ExitStack, contextmanager

import concourse.bass as bass
from concourse import mybir

ALU = mybir.AluOpType
ACT = mybir.ActivationFunctionType
F32 = mybir.dt.float32
F32R = mybir.dt.float32r
I32 = mybir.dt.int32

P = 128
D = 1024
KC = D // P
SEQ, NMETA = 512, 16
L = SEQ + NMETA
LH = L // 2
LPAD = 640
ALPHA = 4.0 ** 0.25
LN_EPS = 1e-5
RMS_EPS = 1e-6
SLOT = 2048
CH = 4
NCH = L // CH
NBLK = 5
NPAIR = 4
HGC = 9
MAGIC = 12582912.0
TWO_PI = (6.28125, 0.0019350051879882812, 3.0199159819e-07)
INV_TWO_PI = 0.15915494309189535

STAGES = {}


def _plan():
    slot = tile = 0
    for name, slots, per in [
        ("uqk", 6, 2), ("v", 2, NBLK), ("glu", 1, 4), ("out_ab", 4, 2),
        ("up00", 8, 2), ("down00", 8, 1), ("up01", 8, 2), ("down01", 8, 1),
        ("i", 4, NBLK), ("f", 4, 2), ("q", 4, 2), ("g", 4, 2), ("out_c", 4, 2),
        ("up10", 8, 2), ("down10", 8, 1), ("up11", 8, 2), ("down11", 8, 1),
    ]:
        STAGES[name] = (slot, slots, tile, per)
        slot += slots
        tile += slots * per
    return slot


NSLOT = _plan()


def tmp_tiles(before):
    names = list(STAGES)
    return sum(STAGES[n][1] * STAGES[n][3] for n in names[:names.index(before)] if n not in ("uqk", "v", "i"))


FREE = 1
NROWS = 13


class Chain:

    def __init__(self, eng, sem):
        self.eng, self.sem, self.base, self.count, self.turn = eng, sem, 0, 0, 0

    def step(self, ins):
        ins.then_inc(self.sem, 1)
        self.count += 1

    def settle(self):
        self.eng.wait_ge(self.sem, self.turn + (self.base + self.count))

    @contextmanager
    def loop(self, turns, per):
        self.base, self.count = self.base + self.count, 0
        with self.eng.Fori(0, turns) as i:
            self.turn = i * per
            yield i
        assert self.count == per, (self.count, per)
        self.base, self.count, self.turn = self.base + turns * per, 0, 0


def trunk(nc, x, meta, w_in_ab, s5_lam_re, s5_lam_im, s5_log_dt, s5_b_re, s5_b_im, s5_c_re, s5_c_im,
          s5_d, s5_w_glu, s5_b_glu, w_out_ab, w_in_c, hgrn_gamma, hgrn_norm_g, w_out_c,
          ln_mix_g, ln_mix_b, mlp_w_up, mlp_b_up, mlp_w_down, mlp_b_down, ln_mlp_g, ln_mlp_b, out):
    with ExitStack() as ctx:
        def sb(name, shape, dt=F32, where=ctx):
            return where.enter_context(nc.sbuf_tensor(name, shape, dt))

        def sem(name):
            return ctx.enter_context(nc.semaphore(name))

        h = sb("h", [P, KC, L])
        mi = ExitStack()
        btt = sb("btt", [P, 2, 4, P], F32, mi)
        kt = sb("kt", [P, 2, 4, CH, 32], F32, mi)
        bt = sb("bt", [P, 2, 4, CH, 32], F32, mi)
        b0r = sb("b0r", [P, 2, 4, CH, 32], F32, mi)
        cm = sb("cm", [P, 2, 2, 4, 5, 32], F32, mi)
        ss = sb("ss", [P, 2, 2, 4, NCH + 1], F32, mi)
        mi.close()
        hh = sb("hh", [P, KC, LPAD], F32R)
        hl = sb("hl", [P, KC, LPAD], F32R)
        raw = sb("raw", [P, 2, SLOT])
        wh = sb("wh", [P, 2, SLOT], F32R)
        wl = sb("wl", [P, 2, SLOT], F32R)
        tmp = sb("tmp", [P, 2, L])
        tmq = sb("tmq", [P, 2, L])
        total = sb("total", [P, L])
        ident = sb("ident", [P, P])
        mean_w = sb("mean_w", [P, P])
        cols_a = sb("cols_a", [P, P])
        cols_b = sb("cols_b", [P, 112])
        uqk_scale = sb("uqk_scale", [P, 3])
        nb_glu = sb("nb_glu", [P, 4])
        lbp = sb("lbp", [P, 8, 8])

        m0 = ExitStack()
        uqk = sb("uqk", [P, 12, L], F32, m0)
        v0 = sb("v0", [P, NBLK, 512], F32, m0)
        m0a = ExitStack()
        pw = sb("pw", [P, 2, 16, 5], F32, m0a)
        bb = sb("bb", [P, 2, 16, 16], F32, m0a)
        cn = sb("cn", [P, 2, 4, 2, 64], F32, m0a)
        co = sb("co", [P, 2, 16, 16], F32, m0a)
        lin_a = sb("lin_a", [P, P], F32, m0a)
        lin_b = sb("lin_b", [112, P], F32, m0a)
        ldt = sb("ldt", [112, 2], F32, m0a)
        pt = sb("pt", [P, 26, 16], F32, m0a)
        wb = sb("wb", [P, 2, 16, CH, 16], F32, m0a)
        wc = sb("wc", [P, 2, 16, 5, 16], F32, m0a)
        group = sb("group", [P, 2], F32, m0a)
        ew = sb("ew", [P, 5, 16], F32, m0a)
        m0x = ExitStack()
        x_tok = sb("x_tok", [P, 4, D], F32, m0x)
        meta_tok = sb("meta_tok", [NMETA, D], F32, m0x)
        m0x.close()
        er = sb("er", [P, 16, NCH], F32, m0a)
        ei = sb("ei", [P, 16, NCH], F32, m0a)
        vq = sb("vq", [P, 4, 4, NCH], F32, m0a)
        m0a.close()
        m0b = ExitStack()
        ntri = sb("ntri", [P, P], F32, m0b)
        nones = sb("nones", [P, P], F32, m0b)
        vis = sb("vis", [P, P], F32, m0b)
        qs = sb("qs", [P, L], F32, m0b)
        ks = sb("ks", [P, LPAD], F32, m0b)
        vs = sb("vs", [P, NBLK, P], F32, m0b)
        al = sb("al", [P, 2, 512], F32, m0b)
        SPO = [0, 80, 208, 464, 848]
        sp = sb("sp", [P, 2, 1360], F32, m0b)
        w_att = sb("w_att", [P, 2, 512], F32, m0b)
        m0b.close()
        m0.close()
        def carve(src, at, shape):
            n = 1
            for k in shape:
                n *= k
            names = [f"a{k}" for k in range(len(shape))]
            return src[:, at:at + n].rearrange(f"p ({' '.join(names)}) -> p {' '.join(names)}", **dict(zip(names, shape)))
        ga, ge = tmq[:, 0, :], tmq[:, 1, :]
        uj = [w.rearrange("p (a c) -> p a c", a=4)
              for w in (tmp[:, 0, :], tmp[:, 1, :], total[:, :])]
        rt = [tmq[:, par, :].rearrange("p (a c) -> p a c", a=4) for par in range(2)]

        m1 = ExitStack()
        v1 = sb("v1", [P, NBLK, D], F32, m1)
        kd = sb("kd", [P, 8, L], F32, m1)
        qd = sb("qd", [P, 8, L], F32, m1)
        gs = sb("gs", [P, 8, L], F32, m1)
        elast = sb("elast", [P, 8, HGC], F32, m1)
        sg = sb("sg", [P, L], F32, m1)
        bc = sb("bc", [P, L], F32, m1)
        elz = sb("elz", [P, 8, 8], F32, m1)
        vh = sb("vh", [P, NBLK, P], F32, m1)
        kdt = sb("kdt", [P, NBLK, P], F32, m1)
        sct = sb("sct", [P, NBLK, P], F32, m1)
        d1 = sb("d1", [P, P, 8], F32, m1)
        same = sb("same", [P, P], F32, m1)
        rms_w = sb("rms_w", [P, P], F32, m1)
        m1f = ExitStack()
        keep = sb("keep", [P, L], F32, m1f)
        lf = sb("lf", [P, L], F32, m1f)
        m1f.close()
        d0 = sb("d0", [P, P, 8], F32, m1)
        m1.close()

        m2 = ExitStack()
        hidh = sb("hidh", [P, 16, L], F32R, m2)
        hidl = sb("hidl", [P, 16, L], F32R, m2)
        m2.close()
        m3 = ExitStack()
        o_tok = sb("o_tok", [P, 4, D], F32, m3)
        m3.close()

        pb = ctx.enter_context(nc.psum_tensor("pb", [P, 8, 512], F32))

        def dense(t):
            b = 2 * (t % 2)
            return pb[:, b:b + 2, 0:LH]

        def halves(ap):
            return ap.rearrange("p (a c) -> p a c", a=2)

        rows_in = sem("rows_in")
        bc_in = sem("bc_in")
        x_in = sem("x_in")
        w_in = [sem("w_in_even"), sem("w_in_odd")]
        w_hi = sem("w_hi")
        w_lo = sem("w_lo")
        tile_done = sem("tile_done")
        evac = sem("evac")
        tmp_free = sem("tmp_free")
        consts = sem("consts")
        att_consts = sem("att_consts")
        act_self = sem("act_self")
        dve_self = sem("dve_self")
        xt_done = sem("xt_done")
        xt_hi = sem("xt_hi")
        xt_res = sem("xt_res")
        ready = sem("ready")
        mix_hi = sem("mix_hi")
        mix_ready = sem("mix_ready")
        hid_ready = sem("hid_ready")
        summed = sem("summed")
        ln_mean = sem("ln_mean")
        centred = sem("centred")
        squared = sem("squared")
        sq_summed = sem("sq_summed")
        var_out = sem("var_out")
        ms_out = sem("ms_out")
        guessed = sem("guessed")
        scaled = sem("scaled")
        ln_hi = sem("ln_hi")
        ln_out = sem("ln_out")
        rows_set = sem("rows_set")
        rows_t = sem("rows_t")
        par_dve = sem("par_dve")
        par_act = sem("par_act")
        c_turned = sem("c_turned")
        wb_ready = sem("wb_ready")
        wc_ready = sem("wc_ready")
        zeroed = sem("zeroed")
        bt_ready = sem("bt_ready")
        uj_ready = sem("uj_ready")
        cm_ready = sem("cm_ready")
        bt_turned = sem("bt_turned")
        btt_copied = sem("btt_copied")
        added = sem("added")
        rotated = sem("rotated")
        kern_done = sem("kern_done")
        kt_copied = sem("kt_copied")
        ss_ready = sem("ss_ready")
        y_done = sem("y_done")
        s5_y = sem("s5_y")
        ge_in = sem("ge_in")
        ge_tanh = sem("ge_tanh")
        ge_step = sem("ge_step")
        y_ready = sem("y_ready")
        gate_ready = sem("gate_ready")
        glu_out = sem("glu_out")
        ks_staged = sem("ks_staged")
        vs_staged = sem("vs_staged")
        z_ready = sem("z_ready")
        l_ready = sem("l_ready")
        sp_ready = sem("sp_ready")
        acc_ready = sem("acc_ready")
        w_ready = sem("w_ready")
        wm_ready = sem("wm_ready")
        pv_done = sem("pv_done")
        o_hi = sem("o_hi")
        o_evac = sem("o_evac")
        hmask = sem("hmask")
        f_ln = sem("f_ln")
        f_b = sem("f_b")
        f_exp = sem("f_exp")
        f_kd = sem("f_kd")
        q_done = sem("q_done")
        g_exp = sem("g_exp")
        g_done = sem("g_done")
        k_staged = sem("k_staged")
        v_staged = sem("v_staged")
        k_turned = sem("k_turned")
        scored = sem("scored")
        kv_done = sem("kv_done")
        o_done = sem("o_done")
        ms_done = sem("ms_done")
        kdt_ready = sem("kdt_ready")
        o_out = sem("o_out")
        sct_ready = sem("sct_ready")
        d_ready = sem("d_ready")
        states_ready = sem("states_ready")
        ho = sem("ho")
        ot_done = sem("ot_done")
        ot_copied = sem("ot_copied")
        out_sem = sem("out_sem")

        block = ctx.enter_context(nc.Block())

        halves_of = [slice(0, 64), slice(64, 128)]

        def k_major(w, cols, kcs=KC):
            return w.rearrange("(k p) n -> p k n", p=P)[:, 0:kcs, cols]

        @block.sync
        def _(sp_):
            def load(i, c, src, kcs=KC):
                sp_.wait_ge(w_lo, i * 2 + (c - 1))
                sp_.dma_start(raw[:, c % 2, :].rearrange("p (k n) -> p k n", k=kcs), src).then_inc(w_in[c % 2], 16)

            def stream(name, w, cols, kcs, col0=0, skip=0):
                s0, slots, _, _ = STAGES[name]
                wv = w.rearrange("(k p) n -> p k n", p=P)
                with sp_.Fori(0, (slots - skip) // 2) as i:
                    for j in range(2):
                        load(i, s0 + skip + j, wv[:, :, bass.ds(i * (2 * cols) + (col0 + (skip + j) * cols), cols)], kcs)

            sp_.dma_start(x_tok[:, :, :], x[0].rearrange("(t p) d -> p t d", p=P)).then_inc(x_in, 16)
            sp_.dma_start(meta_tok[:, :], meta).then_inc(x_in, 16)
            wv = w_in_ab[0].rearrange("(k p) n -> p k n", p=P)
            for s in range(2):
                sp_.dma_start(raw[:, s, :].rearrange("p (k n) -> p k n", k=KC),
                              wv[:, :, s * 256:(s + 1) * 256]).then_inc(w_in[s], 16)
            stream("uqk", w_in_ab[0], 256, KC, skip=2)
            stream("v", w_in_ab[0], 256, KC, col0=1536)
            s0 = STAGES["glu"][0]
            load(0, s0, s5_w_glu[0].rearrange("(k p) n -> p k n", p=P), 4)
            stream("out_ab", w_out_ab[0], 256, KC)

            def mlp(layer):
                for half in range(2):
                    stream(f"up{layer}{half}", mlp_w_up[layer], 256, KC, col0=2048 * half)
                    stream(f"down{layer}{half}", mlp_w_down[layer][2048 * half:2048 * (half + 1), :], P, 16)

            mlp(0)
            stream("i", w_in_c[0], 256, KC, col0=2 * D)
            stream("f", w_in_c[0], 256, KC, col0=D)
            stream("q", w_in_c[0], 256, KC, col0=0)
            stream("g", w_in_c[0], 256, KC, col0=3 * D)
            stream("out_c", w_out_c[0], 256, KC)
            mlp(1)
            for t in range(4):
                sp_.wait_ge(ot_copied, t + 1)
                sp_.dma_start(out[0, t * P:(t + 1) * P, :], o_tok[:, t, :]).then_inc(out_sem, 16)
            sp_.wait_ge(out_sem, 16 * 4)

        @block.gpsimd
        def _(pool):
            def low(s, par):
                pool.wait_ge(w_hi, s + 1)
                pool.tensor_tensor(wl[:, par, :], raw[:, par, :], wh[:, par, :].bitcast(F32),
                                   ALU.subtract).then_inc(w_lo, 1)

            pool.memset(ident[:, :], 0.0).then_inc(consts, 1)
            pool.wait_ge(consts, 1)
            pool.affine_select(out=ident[:, :], in_=ident[:, :], compare_op=ALU.not_equal, fill=1.0,
                               base=0, pattern=[[-1, P]], channel_multiplier=1).then_inc(consts, 1)
            pool.memset(mean_w[:, :], 1.0 / D).then_inc(consts, 1)
            pool.memset(uqk_scale[:, 0:3:2], 1.0).then_inc(consts, 1)
            pool.memset(uqk_scale[:, 1:2], 64.0 ** -0.5).then_inc(consts, 1)
            pool.memset(hh[:, :, L:LPAD].bitcast(F32), 0.0).then_inc(consts, 1)
            pool.memset(hl[:, :, L:LPAD].bitcast(F32), 0.0).then_inc(consts, 1)
            low(0, 0)
            low(1, 1)

            def lows(name, pairs=None):
                s0, slots, _, _ = STAGES[name]
                with pool.Fori(0, pairs if pairs is not None else slots // 2) as i:
                    for j in range(2):
                        low(i * 2 + (s0 + 2 + j), (s0 + j) % 2)

            def decays(q):
                pool.memset(rt[q % 2][:, :, 0:1], 0.0)
                return pool.tensor_copy(rt[q % 2][:, :, 1:NCH],
                                        pt[:, 18, 4 * q:4 * q + 4].unsqueeze(2).broadcast_to([P, 4, NCH - 1]))

            def blocks(o, x_, n):
                return pool.tensor_tensor(o.rearrange("p a k (g c) -> p (a k) g c", g=2),
                                          x_.rearrange("p a k c -> p (a k) c").unsqueeze(2).broadcast_to([P, n, 2, 16]),
                                          group[:, :].unsqueeze(1).unsqueeze(3).broadcast_to([P, n, 2, 16]), ALU.mult)

            def b_blocks(q):
                for ri in range(2):
                    ins = blocks(bt[:, ri], wb[:, ri, 4 * q:4 * q + 4], 4 * CH)
                ins.then_inc(bt_ready, 1)
                pool.wait_ge(bt_ready, q + 1)
                for ri in range(2):
                    for k in range(CH):
                        ins = pool.tensor_copy(b0r[:, ri, :, k, :], bt[:, ri, :, 0, :])
                return ins

            def c_blocks(q):
                for ri in range(2):
                    ins = blocks(cm[:, q % 2, ri], wc[:, ri, 4 * q:4 * q + 4], 4 * 5)
                return ins

            lows("uqk")
            lows("v")
            pool.wait_ge(tile_done, STAGES["glu"][2])
            pool.memset(kt[:, :, :, :, :].rearrange("p a b c d -> p (a b c d)"), 0.0).then_inc(zeroed, 1)
            pool.wait_ge(wb_ready, 1)
            b_blocks(0)
            pool.wait_ge(wc_ready, 1)
            decays(0)
            c_blocks(0).then_inc(cm_ready, 1)
            def stage_pair(i):
                if i:
                    pool.wait_ge(z_ready, i * 10)
                pool.tensor_copy(qs[:, :], uqk[:, i + 4, :]).then_inc(ks_staged, 1)
                pool.tensor_copy(ks[:, 0:L], uqk[:, i + 8, :]).then_inc(ks_staged, 1)
                if i:
                    pool.wait_ge(pv_done, i * 10 + FREE)
                pool.tensor_copy(vs[:, :, :], v0[:, :, i * P:(i + 1) * P]).then_inc(vs_staged, 1)

            for q in range(1, 4):
                if q == 2:
                    pool.memset(ntri[:, :], -1.0).then_inc(att_consts, 1)
                    pool.memset(nones[:, :], -1.0).then_inc(att_consts, 1)
                    pool.memset(vis[:, :], 1.0).then_inc(att_consts, 1)
                    pool.memset(ks[:, L:LPAD], 0.0).then_inc(att_consts, 1)
                    pool.wait_ge(att_consts, 4)
                    pool.affine_select(out=ntri[:, :], in_=ntri[:, :], compare_op=ALU.is_ge, fill=0.0,
                                       base=0, pattern=[[-1, P]], channel_multiplier=1).then_inc(att_consts, 1)
                    pool.affine_select(out=vis[:, :], in_=vis[:, :], compare_op=ALU.is_gt, fill=0.0,
                                       base=0, pattern=[[1, P]], channel_multiplier=-1).then_inc(att_consts, 1)
                    stage_pair(0)
                pool.wait_ge(bt_turned, q)
                pool.wait_ge(kern_done, q)
                b_blocks(q)
                if q >= 2:
                    pool.wait_ge(y_done, q - 1)
                    pool.wait_ge(ss_ready, q - 1)
                decays(q)
                c_blocks(q).then_inc(cm_ready, 1)
            for i in range(NPAIR):
                if i:
                    stage_pair(i)
                y = uqk[:, i, :]
                pool.wait_ge(s5_y, 4 + FREE)
                pool.tensor_tensor(ga[:, :], y, y, ALU.mult).then_inc(ge_step, 1)
                pool.wait_ge(ge_step, i * 5 + 1)
                pool.tensor_scalar(ga[:, :], ga[:, :], 0.044715, 1.0, ALU.mult, ALU.add).then_inc(ge_step, 1)
                pool.wait_ge(ge_step, i * 5 + 2)
                pool.tensor_tensor(ga[:, :], ga[:, :], y, ALU.mult).then_inc(ge_in, 1)
                pool.wait_ge(ge_tanh, i + 1)
                pool.tensor_scalar(ge[:, :], ge[:, :], 1.0, 0.5, ALU.add, ALU.mult).then_inc(ge_step, 1)
                pool.wait_ge(ge_step, i * 5 + 3)
                pool.tensor_tensor(y, y, ge[:, :], ALU.mult).then_inc(ge_step, 1)
                pool.wait_ge(ge_step, i * 5 + 4)
                yh = hh[:, i, 0:L]
                pool.tensor_copy(yh, y).then_inc(ge_step, 1)
                pool.wait_ge(ge_step, i * 5 + 5)
                pool.tensor_tensor(hl[:, i, 0:L], y, yh.bitcast(F32), ALU.subtract).then_inc(y_ready, 1)
            low(STAGES["glu"][0] + 2, 0)
            for name in ["out_ab", "up00", "down00", "up01", "down01", "i", "f", "q", "g"]:
                lows(name)
            pool.wait_ge(hmask, 1)
            pool.wait_ge(tmp_free, tmp_tiles("out_c") + 2)
            pool.affine_select(out=same[:, :], in_=same[:, :], compare_op=ALU.is_ge, fill=0.0,
                               base=0, pattern=[[1, P]], channel_multiplier=-1).then_inc(consts, 1)
            with pool.Fori(0, 8) as i:
                pool.wait_ge(scored, i + FREE)
                pool.tensor_copy(tmp[:, 0, :], kd[:, bass.ds(i, 1), :]).then_inc(k_staged, 1)
                pool.wait_ge(o_done, i + FREE)
                pool.tensor_copy(vh[:, :, :], v1[:, :, bass.ds(i * P, P)]).then_inc(v_staged, 1)
            for name in ["out_c", "up10", "down10", "up11"]:
                lows(name)
            lows("down11", 3)

        @block.tensor
        def _(pe):
            pe.sem_inc(pv_done, FREE)
            pe.sem_inc(scored, FREE)
            pe.sem_inc(o_done, FREE)

            def prods(o, par, w0, w1, rh, rl, kc, first, last):
                lh, ll = wh[:, par, w0:w1], wl[:, par, w0:w1]
                for b in range(2):
                    pe.matmul(o[:, b, :], lh, rh[:, kc, b * LH:(b + 1) * LH], start=first, stop=False)
                for b in range(2):
                    pe.matmul(o[:, b, :], lh, rl[:, kc, b * LH:(b + 1) * LH], start=False, stop=False)
                for b in range(2):
                    mm = pe.matmul(o[:, b, :], ll, rh[:, kc, b * LH:(b + 1) * LH], start=False, stop=last)
                return mm

            def slot_tiles(s, par, t, t_par, per, kcs, cols, rh, rl, chunk_ready, order=None):
                pe.wait_ge(w_lo, s + 1)
                for j in range(per):
                    pe.wait_ge(evac, t + (j + 1))
                    for n, kc in enumerate(order or range(kcs)):
                        if j == 0 and chunk_ready:
                            pe.wait_ge(chunk_ready[0], chunk_ready[1] + n + 1)
                        w0 = kc * cols + j * P
                        mm = prods(dense(t_par + j), par, w0, w0 + P, rh, rl, kc, n == 0, n == kcs - 1)
                    mm.then_inc(tile_done, 1)

            def run(name, kcs, cols, rh, rl, chunk_ready, order=None):
                s0, slots, t0, per = STAGES[name]
                with pe.Fori(0, slots // 2) as i:
                    for j in range(2):
                        slot_tiles(i * 2 + (s0 + j), (s0 + j) % 2, i * (2 * per) + (t0 + j * per), t0 + j * per,
                                   per, kcs, cols, rh, rl, chunk_ready, order)

            def run_tok(name, starts):
                s0, slots, t0, per = STAGES[name]
                with pe.Fori(0, slots // 2) as i:
                    for j in range(2):
                        par = (s0 + j) % 2
                        pe.wait_ge(w_lo, i * 2 + (s0 + j + 1))
                        for k, a in enumerate(starts):
                            t = t0 + j * per + k
                            pe.wait_ge(evac, i * (2 * per) + (t + 1))
                            o = pb[:, 2 * (t % 2), 0:256]
                            for kc in range(KC):
                                w = slice(kc * 256, (kc + 1) * 256)
                                if name == "i" and k == 0:
                                    pe.wait_ge(ready, 16 + kc + 1)
                                pe.matmul(o, hh[:, kc, a:a + P], wh[:, par, w], start=kc == 0, stop=False)
                                pe.matmul(o, hh[:, kc, a:a + P], wl[:, par, w], start=False, stop=False)
                                mm = pe.matmul(o, hl[:, kc, a:a + P], wh[:, par, w], start=False, stop=kc == KC - 1)
                            mm.then_inc(tile_done, 1)

            def layer_norm(n):
                pe.wait_ge(summed, 8 * (n + 1) + FREE)
                for b in range(2):
                    mm = pe.matmul(pb[:, 4 + b, 0:LH], mean_w[:, :], total[:, b * LH:(b + 1) * LH],
                                   start=True, stop=True)
                mm.then_inc(ln_mean, 1)
                for m in range(KC):
                    pe.wait_ge(squared, 8 * n + m + 1)
                    for b in range(2):
                        mm = pe.matmul(pb[:, 6 + b, 0:LH], mean_w[:, :], tmq[:, m % 2, b * LH:(b + 1) * LH],
                                       start=m == 0, stop=m == KC - 1)
                    mm.then_inc(sq_summed, 1)

            def mlp(layer, n):
                for half in range(2):
                    run(f"up{layer}{half}", KC, 256, hh, hl, (ready, 8 * (n + 1)))
                    run(f"down{layer}{half}", 16, P, hidh, hidl, (hid_ready, 16 * (2 * layer + half)))

            pe.wait_ge(consts, 2)
            pe.wait_ge(rows_in, 16 * NROWS)
            pe.wait_ge(rows_set, 2)
            pe.transpose(pb[:, 4, 0:P], lin_a[:, :], ident[:, :])
            pe.transpose(pb[:, 5, 0:112], lin_b[:, :], ident[0:112, 0:112]).then_inc(rows_t, 1)
            pe.wait_ge(x_in, 32)
            for kc in range(KC):
                if kc >= 2:
                    pe.wait_ge(xt_res, 2 * (kc - 1))
                b = 2 * (kc % 2)
                pe.transpose(pb[:, b, 0:NMETA], meta_tok[:, kc * P:(kc + 1) * P], ident[0:NMETA, 0:NMETA])
                for t in range(4):
                    o = pb[:, b, NMETA + t * P:NMETA + (t + 1) * P] if t < 3 else pb[:, b + 1, 0:P]
                    mm = pe.transpose(o, x_tok[:, t, kc * P:(kc + 1) * P], ident[:, :])
                mm.then_inc(xt_done, 1)
            pe.wait_ge(xt_res, 16)
            pe.wait_ge(consts, 7)
            run("uqk", KC, 256, hh, hl, (ready, 0))
            pe.wait_ge(bc_in, 16 * 6)
            for ri in range(2):
                for q in range(4):
                    mm = pe.transpose(pb[:, 6 + ri, q * P:(q + 1) * P], cn[:, ri, q].rearrange("p d c -> p (d c)"),
                                      ident[:, :])
            mm.then_inc(c_turned, 1)
            run_tok("v", [b * P for b in range(NBLK)])

            pe.wait_ge(evac, STAGES["glu"][2] + 2)

            def turn_b(q):
                pe.wait_ge(bt_ready, q + 1)
                if q:
                    pe.wait_ge(kt_copied, q)
                for ri in range(2):
                    for p in range(4):
                        mm = pe.transpose(pb[:, 4 + ri, p * P:(p + 1) * P],
                                          bt[:, ri, p].rearrange("p a b -> p (a b)"), ident[:, :])
                mm.then_inc(bt_turned, 1)

            def outputs(q):
                pe.wait_ge(ss_ready, q + 1)
                pe.wait_ge(kt_copied, q + 1)
                if q:
                    pe.wait_ge(s5_y, q + FREE)
                for p in range(4):
                    o = pb[:, 6 + p // 2, (p % 2) * NCH:(p % 2 + 1) * NCH]
                    pe.matmul(o, kt[:, q % 2, p].rearrange("p a b -> p (a b)"), uj[q % 3][:, p, :],
                              start=p % 2 == 0, stop=False, skip_group_check=True)
                    for ri in range(2):
                        mm = pe.matmul(o, cm[:, q % 2, ri, p, 1:5].rearrange("p a b -> p (a b)"),
                                       ss[:, q % 2, ri, p, 0:NCH],
                                       start=False, stop=(p % 2 == 1 and ri == 1), skip_group_check=True)
                mm.then_inc(y_done, 1)

            turn_b(0)
            for q in range(4):
                pe.wait_ge(btt_copied, q + 1)
                pe.wait_ge(uj_ready, q + 1)
                if q:
                    pe.wait_ge(rotated, q)
                for ri in range(2):
                    for p in range(4):
                        mm = pe.matmul(pb[:, 2 * ri + p // 2, (p % 2) * NCH:(p % 2 + 1) * NCH], btt[:, ri, p, :],
                                       uj[q % 3][:, p, :], start=p % 2 == 0, stop=p % 2 == 1, skip_group_check=True)
                mm.then_inc(added, 1)
                pe.wait_ge(cm_ready, q + 1)
                for p in range(4):
                    for ri in range(2):
                        mm = pe.matmul(pb[:, 4, p * P:(p + 1) * P], b0r[:, ri, p].rearrange("p a b -> p (a b)"),
                                       cm[:, q % 2, ri, p, 0:CH].rearrange("p a b -> p (a b)"),
                                       start=(p == 0 and ri == 0), stop=(p == 3 and ri == 1), skip_group_check=True)
                mm.then_inc(kern_done, 1)
                if q:
                    outputs(q - 1)
                if q < 3:
                    turn_b(q + 1)
            outputs(3)

            pe.wait_ge(att_consts, 6)
            pe.wait_ge(rotated, 4)
            pe.wait_ge(kt_copied, 4)

            def unit(n):
                return divmod(n, 5)

            def z(i, n):
                hd, u = unit(n)
                ps = slice(64 * hd, 64 * hd + 64)
                if n >= 5:
                    pe.wait_ge(w_ready, i * 10 + (n - 4))
                if u == 0:
                    for b in range(NBLK):
                        mm = pe.matmul(pb[:, 0, 16 * b:16 * b + 16], ks[ps, b * P:(b + 1) * P], qs[ps, 512:L],
                                       start=b == 0, stop=b == NBLK - 1, skip_group_check=True)
                else:
                    b = 4 - u
                    mm = pe.matmul(pb[:, u, 0:P * u], ks[ps, b * P:(b + 1) * P], qs[ps, b * P:512],
                                   start=True, stop=True)
                mm.then_inc(z_ready, 1)

            def acc(i, n):
                hd, u = unit(n)
                pe.wait_ge(sp_ready, i * 10 + (n + 1))
                pe.wait_ge(l_ready, i * 10 + (n + 1))
                s = sp[:, hd, SPO[u]:SPO[u] + (80 if u == 0 else P * u)]
                mm = pe.matmul(pb[:, u, 0:80 if u == 0 else P * u], ntri[:, :], s, start=False, stop=False,
                               skip_group_check=True)
                if u == 0:
                    for dd in range(1, NBLK):
                        mm = pe.matmul(pb[:, 0, 0:80 - 16 * dd], nones[:, :], sp[:, hd, 16 * dd:80],
                                       start=False, stop=dd == NBLK - 1, skip_group_check=True)
                for v in range(1, u):
                    mm = pe.matmul(pb[:, u, P * (u - v):P * u], nones[:, :], sp[:, hd, SPO[v]:SPO[v] + P * v],
                                   start=False, stop=v == u - 1, skip_group_check=True)
                mm.then_inc(acc_ready, 1)

            def pv(i, n):
                hd, u = unit(n)
                pe.wait_ge(wm_ready, i * 10 + (n + 1))
                if n == 0:
                    pe.wait_ge(vs_staged, i + 1)
                    pe.wait_ge(s5_y, 4 + FREE)
                if u == 0:
                    pe.wait_ge(o_evac, i * 4 + 2 * hd + FREE)
                    for b in range(NBLK):
                        mm = pe.matmul(pb[64 * hd:64 * hd + 64, 7, 0:16], vs[:, b, 64 * hd:64 * hd + 64],
                                       w_att[:, n % 2, 16 * b:16 * b + 16], start=b == 0, stop=b == NBLK - 1,
                                       skip_group_check=True)
                else:
                    b = 4 - u
                    mm = pe.matmul(pb[64 * hd:64 * hd + 64, 5 + hd, b * P:512], vs[:, b, 64 * hd:64 * hd + 64],
                                   w_att[:, n % 2, 0:P * u], start=u == 1, stop=u == 4, skip_group_check=True)
                mm.then_inc(pv_done, 1)

            def pair(i, last):
                for n in range(10):
                    if n < 9:
                        z(i, n + 1)
                    acc(i, n)
                    if n >= 1:
                        pv(i, n - 1)
                if not last:
                    pe.wait_ge(ks_staged, i * 2 + 4)
                    pe.wait_ge(w_ready, i * 10 + 6)
                    z(i + 1, 0)
                pv(i, 9)

            pe.wait_ge(ks_staged, 2)
            z(0, 0)
            with pe.Fori(0, NPAIR - 1) as i:
                pair(i, False)
            pair(NPAIR - 1, True)

            s0, _, t0, per = STAGES["glu"]
            slot_tiles(s0, s0 % 2, t0, t0, per, 4, 512, hh, hl, (y_ready, 0))
            run("out_ab", KC, 256, hh, hl, (mix_ready, 0), order=[4, 5, 6, 7, 0, 1, 2, 3])
            layer_norm(0)
            mlp(0, 0)
            layer_norm(1)
            run_tok("i", [0] + [NMETA + t * P for t in range(4)])
            run("f", KC, 256, hh, hl, None)
            run("q", KC, 256, hh, hl, None)
            run("g", KC, 256, hh, hl, None)

            def keys(i):
                pe.wait_ge(k_staged, i + 1)
                pe.transpose(pb[0:16, 1, 0:P], tmp[:, 0, 0:16], ident[:, :])
                for t in range(4):
                    mm = pe.transpose(pb[:, 0, t * P:(t + 1) * P], tmp[:, 0, NMETA + t * P:NMETA + (t + 1) * P], ident[:, :])
                mm.then_inc(k_turned, 1)
                pe.matmul(pb[0:16, 5, 0:16], tmp[:, 0, 0:16], qd[:, bass.ds(i, 1), 0:16], start=True, stop=True)
                for t in range(4):
                    mm = pe.matmul(pb[:, 4, t * P:(t + 1) * P], tmp[:, 0, NMETA + t * P:NMETA + (t + 1) * P],
                                   qd[:, bass.ds(i, 1), NMETA + t * P:NMETA + (t + 1) * P],
                                   start=t == 0, stop=t == 3, skip_group_check=True)
                mm.then_inc(scored, 1)

            def chunk_sums(i):
                pe.wait_ge(kdt_ready, i * 2 + 2)
                pe.wait_ge(v_staged, i + 1)
                for c in range(8):
                    k = (c - 1) // 2
                    o = pb[:, 2 + (c + 1) % 2, k * P:(k + 1) * P] if c else pb[:, 1, P:2 * P]
                    if c == 0:
                        lt, rh = kdt[0:16, 0, :], vh[0:16, 0, :]
                    else:
                        t, r = 1 + (c - 1) // 2, 64 * ((c - 1) % 2)
                        lt, rh = kdt[r:r + 64, t, :], vh[r:r + 64, t, :]
                    mm = pe.matmul(o, lt, rh, start=c < 3, stop=c in (0, 6, 7), skip_group_check=True)
                mm.then_inc(kv_done, 1)

            def head_output(i):
                pe.wait_ge(sct_ready, i * 2 + 2)
                pe.wait_ge(ms_out, i * 2 + FREE)
                pe.matmul(pb[:, 7, 0:16], vh[0:16, 0, :], sct[0:16, 0, 0:16], start=True, stop=True)
                for t in range(4):
                    pe.matmul(pb[:, 6, t * P:(t + 1) * P], vh[:, 1 + t, :], sct[:, 1 + t, :],
                              start=t == 0, stop=False, skip_group_check=True)
                pe.wait_ge(states_ready, i + 1)
                for c in range(1, HGC):
                    a = 64 * (c - 1)
                    mm = pe.matmul(pb[:, 6, a:a + 64], d1[:, :, c - 1], qd[:, bass.ds(i, 1), NMETA + a:NMETA + a + 64],
                                   start=False, stop=c == HGC - 1, skip_group_check=True)
                mm.then_inc(o_done, 1)

            def mean_squares(i):
                pe.wait_ge(o_out, i * 4 + 4)
                pe.matmul(pb[:, 7, 64:80], rms_w[:, :], tmq[:, 0, 0:16], start=True, stop=True).then_inc(ms_done, 1)
                pe.matmul(pb[:, 0, :], rms_w[:, :], tmq[:, 0, 16:L], start=True, stop=True).then_inc(ms_done, 1)

            pe.wait_ge(consts, 8)
            pe.wait_ge(q_done, 8)
            pe.wait_ge(evac, STAGES["out_c"][2] + 2)
            keys(0)
            chunk_sums(0)
            with pe.Fori(0, 7) as i:
                head_output(i)
                keys(i + 1)
                pe.wait_ge(kdt_ready, i * 2 + 4)
                mean_squares(i)
                chunk_sums(i + 1)
            head_output(7)
            mean_squares(7)
            pe.wait_ge(ms_out, 16 + FREE)
            run("out_c", KC, 256, hh, hl, (mix_ready, 8))
            layer_norm(2)
            mlp(1, 2)
            layer_norm(3)
            for t in range(4):
                if t == 0:
                    pe.wait_ge(ln_out, 32)
                if t >= 2:
                    pe.wait_ge(ot_copied, t - 1)
                for kc in range(KC):
                    mm = pe.transpose(pb[:, 2 * (t % 2) + kc // 4, (kc % 4) * P:(kc % 4 + 1) * P],
                                      h[:, kc, NMETA + t * P:NMETA + (t + 1) * P], ident[:, :])
                mm.then_inc(ot_done, 1)

        @block.scalar
        def _(act):
            me = Chain(act, act_self)
            exp_ln = "natural_log_exp_and_others"
            act.preload_act_table_set(exp_ln)
            used = [0]

            def high(i, c):
                act.wait_ge(w_in[c % 2], i * 16 + 16 * (c // 2 + 1))
                act.activation(wh[:, c % 2, :], raw[:, c % 2, :], ACT.Copy).then_inc(w_hi, 1)

            def run(name, empty, split=True, pairs=None):
                s0, slots, t0, per = STAGES[name]
                with act.Fori(0, pairs if pairs is not None else slots // 2) as i:
                    for j in range(2):
                        body(name, empty, i, j, s0, t0, per, split)

            def body(name, empty, i, j, s0, t0, per, split):
                for k in range(per):
                    t = j * per + k
                    act.wait_ge(tile_done, i * (2 * per) + (t0 + t + 1))
                    empty(i, t, dense(t0 + t), (t0 + t) % 2).then_inc(evac, 1)
                if split:
                    high(i, s0 + j + 2)

            n = 0
            for k, src in enumerate([ln_mix_g, ln_mix_b, ln_mlp_g, ln_mlp_b]):
                act.dma_start(lin_a[16 * k:16 * k + 16, :], src.rearrange("l (k c) -> (l k) c", c=P)).then_inc(rows_in, 16)
            act.dma_start(lin_a[64:128, :], mlp_b_up.rearrange("l (k c) -> (l k) c", c=P)).then_inc(rows_in, 16)
            act.wait_ge(rows_set, 1)
            for r0, r1, src in [
                (0, 16, s5_lam_re[0].rearrange("(a s) c -> a (s c)", s=2)),
                (16, 32, s5_lam_im[0].rearrange("(a s) c -> a (s c)", s=2)),
                (32, 48, mlp_b_down.rearrange("l (k c) -> (l k) c", c=P)),
                (48, 52, s5_b_glu.rearrange("l (k c) -> (l k) c", c=P)),
                (52, 56, s5_d[0].rearrange("(k g) c -> k (g c)", k=4)),
                (56, 72, hgrn_gamma.rearrange("l (k c) -> (l k) c", c=P)),
                (72, 80, hgrn_norm_g.rearrange("l (k c) -> (l k) c", c=P)),
            ]:
                act.dma_start(lin_b[r0:r1, :], src).then_inc(rows_in, 16)
            act.dma_start(ldt[96:112, :], s5_log_dt[0].rearrange("(a s) -> a s", s=2)).then_inc(rows_in, 16)
            for ri, src in enumerate([s5_b_re, s5_b_im]):
                act.dma_start(bb[:, ri], src[0].rearrange("(a s) p h -> (s p) a h", s=2)).then_inc(bc_in, 16)
            for ri, src in enumerate([s5_c_re, s5_c_im]):
                for dup in range(2):
                    act.dma_start(cn[:, ri, :, dup, :],
                                  src[0].rearrange("(q g) h p -> (g h) q p", q=4)).then_inc(bc_in, 16)
            act.sem_inc(evac, 2)
            act.sem_inc(o_evac, FREE)

            for kc in range(KC):
                act.wait_ge(xt_res, 2 * (kc + 1))
                act.activation(hh[:, kc, 0:L], h[:, kc, :], ACT.Copy).then_inc(xt_hi, 1)
                if kc == 0:
                    high(0, 0)
                    high(0, 1)

            act.wait_ge(par_dve, 1)
            act.activation(pt[:, 0, :], cols_b[:, 96:112], ACT.Exp).then_inc(par_act, 1)
            act.wait_ge(par_dve, 2)
            act.activation(pt[:, 3, :], pt[:, 1, :], ACT.Exp).then_inc(par_act, 1)
            act.activation(lbp[:, 3, :], lbp[:, 1, :], ACT.Exp).then_inc(par_act, 1)
            act.activation(lbp[:, 4, :], lbp[:, 2, :], ACT.Exp).then_inc(par_act, 1)
            act.wait_ge(par_dve, 3)
            act.activation(pt[:, 6, :], pt[:, 5, :], ACT.Sin).then_inc(par_act, 1)
            act.activation(pt[:, 7, :], pt[:, 5, :], ACT.Sin, scale=0.5).then_inc(par_act, 1)
            act.preload_act_table_set(exp_ln)

            def to_uqk(i, t, o, par):
                return act.activation(halves(uqk[:, bass.ds(i * 4 + t, 1), :].squeeze(1)), o, ACT.Identity,
                                      scale=uqk_scale[:, bass.ds(i, 1)])

            def to_tok(dst):
                s_per = NBLK

                def empty(i, t, o, par):
                    j, k = divmod(t, s_per)
                    return act.activation(dst[:, k, bass.ds(i * 512 + j * 256, 256)], pb[:, 2 * par, 0:256], ACT.Copy)
                return empty

            act.wait_ge(consts, 7)
            run("uqk", to_uqk)

            def u_rows(q):
                for p in range(4):
                    ut = uqk[32 * p:32 * p + 32, q, :].rearrange("p (c j) -> p c j", j=CH)
                    for k in range(CH):
                        ins = act.activation(uj[q % 3][32 * k:32 * k + 32, p, :], ut[:, :, CH - 1 - k], ACT.Copy)
                ins.then_inc(uj_ready, 1)
            act.wait_ge(evac, STAGES["v"][2] + 2)
            u_rows(0)
            u_rows(1)
            run("v", to_tok(v0))

            act.wait_ge(zeroed, 1)
            for q in range(4):
                act.wait_ge(bt_turned, q + 1)
                if q:
                    act.wait_ge(added, q)
                for ri in range(2):
                    ins = act.activation(btt[:, ri].rearrange("p a b -> p (a b)"), pb[:, 4 + ri, :], ACT.Copy)
                ins.then_inc(btt_copied, 1)
                act.wait_ge(kern_done, q + 1)
                if q >= 2:
                    act.wait_ge(y_done, q - 1)
                for k in range(CH):
                    ins = act.activation(
                        kt[32 * k:32 * k + 32, q % 2, :, CH - 1 - k:CH, :],
                        pb[32 * k:32 * k + 32, 4, :].rearrange("p (a t c) -> p a t c", a=4, t=CH)[:, :, 0:k + 1, :],
                        ACT.Copy)
                ins.then_inc(kt_copied, 1)
                if q < 2:
                    if q == 1:
                        act.wait_ge(y_done, 1)
                    u_rows(q + 2)

            with me.loop(NPAIR, 20) as i:
                def pre(n):
                    hd, u = divmod(n, 5)
                    c = 80 if u == 0 else P * u
                    a = al[:, n % 2, 0:c]
                    act.wait_ge(z_ready, i * 10 + (n + 1))
                    if n >= 2:
                        act.wait_ge(sp_ready, i * 10 + (n - 1))
                    me.step(act.activation(a, pb[:, u, 0:c], ACT.Abs))
                    me.settle()
                    me.step(act.activation(a, a, ACT.Exp, scale=-1.0))
                    me.settle()
                    act.activation(a, a, ACT.Ln, bias=1.0).then_inc(l_ready, 1)

                def weigh(n):
                    hd, u = divmod(n, 5)
                    c = 80 if u == 0 else P * u
                    act.wait_ge(acc_ready, i * 10 + (n + 1))
                    if n >= 2:
                        act.wait_ge(pv_done, i * 10 + (n - 1 + FREE))
                    act.activation(w_att[:, n % 2, 0:c], pb[:, u, 0:c], ACT.Exp).then_inc(w_ready, 1)

                def outputs(hd):
                    ps = slice(64 * hd, 64 * hd + 64)
                    act.wait_ge(pv_done, i * 10 + (5 * hd + 5) + FREE)
                    act.activation(hh[ps, bass.ds(i + 4, 1), 0:512].squeeze(1), pb[ps, 5 + hd, :], ACT.Copy).then_inc(o_hi, 1)
                    act.activation(hh[ps, bass.ds(i + 4, 1), 512:L].squeeze(1), pb[ps, 7, 0:16], ACT.Copy).then_inc(o_hi, 1)

                for n in range(10):
                    pre(n)
                    if n >= 1:
                        weigh(n - 1)
                    if n == 7:
                        outputs(0)
                    if n == 4:
                        act.wait_ge(ge_in, i + 1)
                        act.activation(ge[:, :], ga[:, :], ACT.Tanh, scale=0.7978845608028654).then_inc(ge_tanh, 1)
                        act.preload_act_table_set(exp_ln)
                weigh(9)
                outputs(1)
            def into_tmp(name, func, **kw):
                first = used[0]
                _, slots, _, per = STAGES[name]
                used[0] += slots * per

                def empty(i, t, o, par):
                    act.wait_ge(tmp_free, i * (2 * per) + (first + t + 1))
                    more = {k: v(i, t) for k, v in kw.items()}
                    return act.activation(halves(tmp[:, par, :]), o, func, **more)
                return empty

            s0, _, t0, per = STAGES["glu"]
            gate_in = into_tmp("glu", ACT.Exp, bias=lambda i, t: nb_glu[:, t:t + 1], scale=lambda i, t: -1.0)
            for m in range(per):
                act.wait_ge(tile_done, t0 + m + 1)
                gate_in(0, m, dense(t0 + m), (t0 + m) % 2).then_inc(evac, 1)
                e = tmp[:, (t0 + m) % 2, :]
                act.wait_ge(evac, t0 + m + 3)
                me.step(act.activation(e, e, ACT.Ln, bias=1.0))
                me.settle()
                act.activation(e, e, ACT.Exp, scale=-1.0).then_inc(gate_ready, 1)
            high(0, s0 + 2)
            for m in range(4):
                act.wait_ge(glu_out, m + 1)
                act.activation(hh[:, m, 0:L], uqk[:, m, :], ACT.Copy).then_inc(mix_hi, 1)
            run("out_ab", into_tmp("out_ab", ACT.Copy))

            def guess_inv_sqrt(x_, o, ready_, n):
                act.wait_ge(ready_, n)
                me.step(act.activation(o, x_, ACT.Ln))
                me.settle()
                act.activation(o, o, ACT.Exp, scale=-0.5).then_inc(guessed, 1)

            def layer_norm(n, last=False):
                layer, which = divmod(n, 2)
                for m in range(KC):
                    act.wait_ge(centred, 8 * n + m + 1)
                    if m >= 2:
                        act.wait_ge(sq_summed, 8 * n + m - 1)
                    act.activation(tmq[:, m % 2, :], h[:, m, :], ACT.Square).then_inc(squared, 1)
                guess_inv_sqrt(total[:, :], tmq[:, 0, :], var_out, n + 1)
                g0, b0 = 32 * which + 8 * layer, 32 * which + 16 + 8 * layer
                for m in range(KC):
                    act.wait_ge(scaled, 8 * n + m + 1)
                    g, b = cols_a[:, g0 + m:g0 + m + 1], cols_a[:, b0 + m:b0 + m + 1]
                    if not last:
                        act.activation(hh[:, m, 0:L], h[:, m, :], ACT.Identity, bias=b, scale=g).then_inc(ln_hi, 1)
                    act.activation(h[:, m, :], h[:, m, :], ACT.Identity, bias=b, scale=g).then_inc(ln_out, 1)

            def mlp(layer, last=False):
                for half in range(2):
                    c0 = 64 + 32 * layer + 16 * half
                    run(f"up{layer}{half}", into_tmp(f"up{layer}{half}", ACT.Relu,
                                                     bias=lambda i, t: cols_a[:, bass.ds(i * 4 + (c0 + t), 1)]))
                    name = f"down{layer}{half}"
                    if half == 0:
                        run(name, into_tmp(name, ACT.Copy))
                    else:
                        empty = into_tmp(name, ACT.Identity,
                                         bias=lambda i, t: cols_b[:, bass.ds(i * 2 + (32 + 8 * layer + t), 1)])
                        if last:
                            run(name, empty, pairs=3)
                            s0, slots, t0, per = STAGES[name]
                            for j in range(2):
                                body(name, empty, 3, j, s0, t0, per, False)
                        else:
                            run(name, empty)

            layer_norm(0)
            mlp(0)
            layer_norm(1)
            run("i", to_tok(v1))

            fi = into_tmp("f", ACT.Exp, scale=lambda i, t: -1.0)

            s0, slots, t0, per = STAGES["f"]
            with me.loop(slots // 2, 8) as i:
                for j in range(2):
                    for k in range(per):
                        t = j * per + k
                        n, par = i * 4 + t, (t0 + t) % 2
                        e = tmp[:, par, :]
                        act.wait_ge(tile_done, i * (2 * per) + (t0 + t + 1))
                        fi(i, t, dense(t0 + t), par).then_inc(evac, 1)
                        act.wait_ge(evac, i * (2 * per) + (t0 + t + 3))
                        me.step(act.activation(e, e, ACT.Ln, bias=1.0))
                        me.settle()
                        me.step(act.activation(e, e, ACT.Exp, scale=-1.0))
                        me.settle()
                        act.activation(lf[:, :], e, ACT.Ln, bias=lbp[:, 5, bass.ds(n, 1)],
                                       scale=lbp[:, 6, bass.ds(n, 1)]).then_inc(f_ln, 1)
                        if k == 1:
                            high(i, s0 + j + 2)
                        act.wait_ge(f_b, n + 1)
                        act.activation(qd[:, bass.ds(n, 1), :].squeeze(1), bc[:, :], ACT.Exp).then_inc(f_exp, 1)
                        act.activation(tmq[:, par, :], bc[:, :], ACT.Exp, scale=-1.0).then_inc(f_exp, 1)
            run("q", into_tmp("q", ACT.Copy))
            gi = into_tmp("g", ACT.Copy)

            def gate(i, t, o, par):
                act.wait_ge(g_done, i * 4 + t + FREE)
                act.activation(halves(tmq[:, 0, :]), o, ACT.Exp, scale=-1.0).then_inc(g_exp, 1)
                return gi(i, t, o, par)
            run("g", gate)

            def take_k(i):
                act.wait_ge(k_turned, i + 1)
                act.activation(kdt[0:16, 0, :], pb[0:16, 1, 0:P], ACT.Copy).then_inc(kdt_ready, 1)
                act.activation(kdt[:, 1:5, :], pb[:, 0, :].rearrange("p (a b) -> p a b", a=4), ACT.Copy).then_inc(kdt_ready, 1)

            def take_o(i):
                act.wait_ge(o_done, i + 1 + FREE)
                act.activation(tmq[:, 0, 16:L], pb[:, 6, :], ACT.Square).then_inc(o_out, 1)
                act.activation(tmq[:, 0, 0:16], pb[:, 7, 0:16], ACT.Square).then_inc(o_out, 1)
                act.activation(total[:, 16:L], pb[:, 6, :], ACT.Copy).then_inc(o_out, 1)
                act.activation(total[:, 0:16], pb[:, 7, 0:16], ACT.Copy).then_inc(o_out, 1)

            def finish(i, at):
                guess_inv_sqrt(sg[:, :], tmq[:, 0, :], ms_out, i * 2 + 2 + FREE)
                act.wait_ge(ho, i + 1)
                act.activation(at, bc[:, :], ACT.Copy).then_inc(mix_hi, 1)

            take_k(0)
            with me.loop(7, 1) as i:
                take_o(i)
                take_k(i + 1)
                finish(i, hh[:, bass.ds(i, 1), 0:L].squeeze(1))
            take_o(7)
            finish(7, hh[:, 7, 0:L])
            run("out_c", into_tmp("out_c", ACT.Copy))
            layer_norm(2)
            mlp(1, last=True)
            layer_norm(3, last=True)

        @block.vector
        def _(dve):
            me = Chain(dve, dve_self)
            TT, TS, STT = dve.tensor_tensor, dve.tensor_scalar, dve.scalar_tensor_tensor
            used = [0]

            def wait_tile(name, i, t):
                _, _, t0, per = STAGES[name]
                dve.wait_ge(evac, i * (2 * per) + (t0 + t + 3))

            dve.memset(lin_b[:, :], 0.0).then_inc(rows_set, 1)
            dve.sem_inc(tmp_free, 2)
            for free in (s5_y, g_done, summed, ms_out):
                dve.sem_inc(free, FREE)
            dve.wait_ge(rows_in, 16 * NROWS)
            dve.wait_ge(rows_set, 1)
            dve.tensor_copy(lin_b[96:112, :].rearrange("a (s c) -> a s c", s=2),
                            ldt[96:112, :].unsqueeze(2).broadcast_to([16, 2, 64])).then_inc(rows_set, 1)
            dve.wait_ge(rows_t, 1)
            me.step(dve.tensor_copy(cols_a[:, :], pb[:, 4, 0:P]))
            dve.tensor_copy(cols_b[:, :], pb[:, 5, 0:112]).then_inc(par_dve, 1)

            dve.wait_ge(consts, 7)
            for kc in range(KC + 1):
                if kc < KC:
                    b = 2 * (kc % 2)
                    dve.wait_ge(xt_done, kc + 1)
                    dve.tensor_copy(h[:, kc, 0:400], pb[:, b, 0:400]).then_inc(xt_res, 1)
                    dve.tensor_copy(h[:, kc, 400:L], pb[:, b + 1, 0:P]).then_inc(xt_res, 1)
                if kc >= 1:
                    m = kc - 1
                    dve.wait_ge(xt_res, 2 * kc)
                    dve.wait_ge(xt_hi, kc)
                    TT(hl[:, m, 0:L], h[:, m, :], hh[:, m, 0:L].bitcast(F32), ALU.subtract).then_inc(ready, 1)

            def T(k):
                return pt[:, k, :]

            def step(ins):
                me.step(ins)
                me.settle()

            lr, li = cols_b[:, 0:16], cols_b[:, 16:32]
            dve.wait_ge(par_dve, 1)
            step(TS(nb_glu[:, :], cols_b[:, 48:52], -1.0, None, ALU.mult))
            g0, g1 = cols_b[:, 56:64], cols_b[:, 64:72]
            step(TT(lbp[:, 0, :], g0, g1, ALU.max))
            step(TT(lbp[:, 1, :], g0, lbp[:, 0, :], ALU.subtract))
            step(TT(lbp[:, 2, :], g1, lbp[:, 0, :], ALU.subtract))
            dve.wait_ge(par_act, 1)
            TT(T(1), lr, T(0), ALU.mult).then_inc(par_dve, 1)
            step(TT(T(2), li, T(0), ALU.mult))
            step(TS(T(4), T(2), INV_TWO_PI, MAGIC, ALU.mult, ALU.add))
            step(TS(T(4), T(4), MAGIC, None, ALU.subtract))
            step(STT(T(5), T(4), -TWO_PI[0], T(2), ALU.mult, ALU.add))
            step(STT(T(5), T(4), -TWO_PI[1], T(5), ALU.mult, ALU.add))
            step(STT(T(5), T(4), -TWO_PI[2], T(5), ALU.mult, ALU.add))
            dve.wait_ge(par_dve, 2)
            TS(T(5), T(5), 3.1415925, -3.1415925, ALU.min, ALU.max).then_inc(par_dve, 1)
            dve.wait_ge(par_act, 4)
            step(TT(lbp[:, 0, :], lbp[:, 3, :], lbp[:, 4, :], ALU.add))
            step(dve.reciprocal(lbp[:, 0, :], lbp[:, 0, :]))
            step(TT(lbp[:, 1, :], lbp[:, 3, :], lbp[:, 0, :], ALU.mult))
            step(TT(lbp[:, 2, :], lbp[:, 4, :], lbp[:, 0, :], ALU.mult))
            step(TT(lbp[:, 5, :], lbp[:, 1, :], lbp[:, 2, :], ALU.add))
            step(TT(lbp[:, 5, :], lbp[:, 5, :], lbp[:, 1, :], ALU.subtract))
            step(TS(lbp[:, 6, :], lbp[:, 5, :], -1.0, 1.0, ALU.mult, ALU.add))
            step(TS(lbp[:, 7, :], lbp[:, 5, :], -1.0, None, ALU.add))
            dve.wait_ge(par_act, 6)
            step(TT(T(8), T(7), T(7), ALU.mult))
            step(TS(T(8), T(8), -2.0, 1.0, ALU.mult, ALU.add))
            step(TT(T(9), T(3), T(8), ALU.mult))
            step(TT(T(10), T(3), T(6), ALU.mult))
            step(TT(T(11), lr, lr, ALU.mult))
            step(TT(T(12), li, li, ALU.mult))
            step(TT(T(11), T(11), T(12), ALU.add))
            step(dve.reciprocal(T(11), T(11)))
            step(TS(T(12), T(9), -1.0, None, ALU.add))
            step(TT(T(13), T(12), lr, ALU.mult))
            step(TT(T(14), T(10), li, ALU.mult))
            step(TT(T(13), T(13), T(14), ALU.add))
            step(TT(T(13), T(13), T(11), ALU.mult))
            step(TT(T(15), T(10), lr, ALU.mult))
            step(TT(T(14), T(12), li, ALU.mult))
            step(TT(T(15), T(15), T(14), ALU.subtract))
            step(TT(T(15), T(15), T(11), ALU.mult))
            PR, PI = (lambda k: pw[:, 0, :, k]), (lambda k: pw[:, 1, :, k])
            step(dve.memset(PR(0), 1.0))
            step(dve.memset(PI(0), 0.0))
            step(dve.tensor_copy(PR(1), T(9)))
            step(dve.tensor_copy(PI(1), T(10)))
            for k, a, b in [(2, 1, 1), (3, 2, 1), (4, 2, 2)]:
                step(TT(T(16), PR(a), PR(b), ALU.mult))
                step(TT(T(17), PI(a), PI(b), ALU.mult))
                step(TT(PR(k), T(16), T(17), ALU.subtract))
                step(TT(T(16), PR(a), PI(b), ALU.mult))
                step(TT(T(17), PI(a), PR(b), ALU.mult))
                step(TT(PI(k), T(16), T(17), ALU.add))
            step(TT(T(18), T(3), T(3), ALU.mult))
            step(TT(T(18), T(18), T(18), ALU.mult))
            c, s = T(8), T(6)
            for k in (19, 21):
                step(TT(T(23), s, s, ALU.mult))
                step(TT(T(k + 1), s, c, ALU.mult))
                step(TS(T(k + 1), T(k + 1), 2.0, None, ALU.mult))
                step(TS(T(k), T(23), -2.0, 1.0, ALU.mult, ALU.add))
                c, s = T(k), T(k + 1)
            dve.wait_ge(bc_in, 16 * 6)
            fr, fi = (T(k).unsqueeze(2).broadcast_to([P, 16, 16]) for k in (13, 15))
            scratch = vq[:, :, :, :].rearrange("p v a c -> p (v a c)")
            u1, u2, u3, u4 = (carve(scratch, 256 * k, [16, 16]) for k in range(4))
            me.step(TT(u1, bb[:, 0], fr, ALU.mult))
            me.step(TT(u2, bb[:, 1], fi, ALU.mult))
            me.step(TT(u3, bb[:, 1], fr, ALU.mult))
            step(TT(u4, bb[:, 0], fi, ALU.mult))
            me.step(TT(bb[:, 0], u1, u2, ALU.subtract))
            step(TT(bb[:, 1], u3, u4, ALU.add))

            def powers_times(o, k1, srcr, srci, neg, done):
                t = carve(scratch, 0, [16, k1, 16])
                pr, pi = (pw[:, k, :, 0:k1].unsqueeze(3).broadcast_to([P, 16, k1, 16]) for k in range(2))
                xr, xi = (v.unsqueeze(2).broadcast_to([P, 16, k1, 16]) for v in (srcr, srci))
                step(TT(o[:, 0], pr, xr, ALU.mult))
                step(TT(t, pi, xi, ALU.mult))
                step(TT(o[:, 0], o[:, 0], t, ALU.subtract))
                step(TT(o[:, 1], pr, xi, ALU.mult))
                step(TT(t, pi, xr, ALU.mult))
                if neg:
                    line1 = o[:, 1].rearrange("p a b c -> p (a b c)")
                    STT(line1, line1, -1.0, t.rearrange("p a b c -> p (a b c)"), ALU.mult, ALU.subtract).then_inc(done, 1)
                else:
                    TT(o[:, 1], o[:, 1], t, ALU.add).then_inc(done, 1)
                dve.wait_ge(done, 1)

            for g, ps in enumerate(halves_of):
                me.step(dve.memset(group[ps, g:g + 1], 1.0))
                me.step(dve.memset(group[ps, 1 - g:2 - g], 0.0))
            me.settle()
            powers_times(wb, CH, bb[:, 0], bb[:, 1], False, wb_ready)
            step(dve.tensor_copy(ew[:, 0:2, :], pt[:, 21:23, :]))
            step(dve.memset(er[:, :, 0:1], 1.0))
            step(dve.memset(ei[:, :, 0:1], 0.0))
            n = 1
            while n < NCH:
                m = min(n, NCH - n)
                wr, wi = (ew[:, k, :].unsqueeze(2).broadcast_to([P, 16, m]) for k in (0, 1))
                a_, b_ = carve(scratch, 0, [16, m]), carve(scratch, 1024, [16, m])
                me.step(TT(a_, er[:, :, 0:m], wr, ALU.mult))
                step(TT(b_, ei[:, :, 0:m], wi, ALU.mult))
                step(TT(er[:, :, n:n + m], a_, b_, ALU.subtract))
                me.step(TT(a_, er[:, :, 0:m], wi, ALU.mult))
                step(TT(b_, ei[:, :, 0:m], wr, ALU.mult))
                step(TT(ei[:, :, n:n + m], a_, b_, ALU.add))
                n *= 2
                if n < NCH:
                    me.step(TT(ew[:, 2, :], ew[:, 0, :], ew[:, 0, :], ALU.mult))
                    me.step(TT(ew[:, 3, :], ew[:, 1, :], ew[:, 1, :], ALU.mult))
                    step(TT(ew[:, 4, :], ew[:, 0, :], ew[:, 1, :], ALU.mult))
                    me.step(TT(ew[:, 0, :], ew[:, 2, :], ew[:, 3, :], ALU.subtract))
                    step(TS(ew[:, 1, :], ew[:, 4, :], 2.0, None, ALU.mult))
            dve.wait_ge(c_turned, 1)
            for ri in range(2):
                for g, ps in enumerate(halves_of):
                    me.step(dve.tensor_copy(co[ps, ri], pb[ps, 6 + ri, :].rearrange("p (a g c) -> p a g c", a=16, g=2)[:, :, g, :]))
            me.settle()
            powers_times(wc, 5, co[:, 0], co[:, 1], True, wc_ready)
            dve.wait_ge(tile_done, STAGES["glu"][2])
            me.step(dve.memset(ss[:, 0, :, :, 0:1], 0.0))
            step(dve.memset(ss[:, 1, :, :, 0:1], 0.0))

            def flat(v):
                return halves(v.rearrange("p a c -> p (a c)"))

            def line(v):
                return v.rearrange("p a c -> p (a c)")

            def outputs(q):
                dve.wait_ge(y_done, q + 1)
                for p in range(4):
                    ps = slice(32 * p, 32 * p + 32)
                    ut = uqk[ps, q, :].rearrange("p (c j) -> p c j", j=CH)
                    for t in range(CH):
                        ins = STT(ut[:, :, t], ut[:, :, t], cols_b[ps, 52 + q:53 + q],
                                  pb[32 * t:32 * t + 32, 6 + p // 2, (p % 2) * NCH:(p % 2 + 1) * NCH],
                                  ALU.mult, ALU.add)
                ins.then_inc(s5_y, 1)

            xr, xi = pb[:, 0:2, 0:LH], pb[:, 2:4, 0:LH]
            va, vb, vc, vd = (vq[:, k] for k in range(4))
            for q in range(4):
                eq, fq = er[:, 4 * q:4 * q + 4, :], ei[:, 4 * q:4 * q + 4, :]
                sr, si = (ss[:, q % 2, k, :, 1:NCH + 1] for k in range(2))
                dve.wait_ge(added, q + 1)
                me.step(TT(flat(va), flat(eq), xr, ALU.mult))
                me.step(TT(flat(vb), flat(fq), xi, ALU.mult))
                me.step(TT(flat(vc), flat(eq), xi, ALU.mult))
                TT(flat(vd), flat(fq), xr, ALU.mult).then_inc(rotated, 1)
                dve.wait_ge(rotated, q + 1)
                me.step(TT(va, va, vb, ALU.add))
                step(TT(vc, vc, vd, ALU.subtract))
                dve.wait_ge(cm_ready, q + 1)
                me.step(dve.tensor_tensor_scan(line(vb), line(rt[q % 2]), line(va), 0.0, ALU.mult, ALU.add))
                step(dve.tensor_tensor_scan(line(vd), line(rt[q % 2]), line(vc), 0.0, ALU.mult, ALU.add))
                if q >= 2:
                    dve.wait_ge(y_done, q - 1)
                me.step(TT(va, eq, vb, ALU.mult))
                step(TT(vc, fq, vd, ALU.mult))
                step(TT(sr, va, vc, ALU.subtract))
                me.step(TT(va, eq, vd, ALU.mult))
                step(TT(vc, fq, vb, ALU.mult))
                TT(si, va, vc, ALU.add).then_inc(ss_ready, 1)
                dve.wait_ge(ss_ready, q + 1)
                if q:
                    outputs(q - 1)
            outputs(3)

            dve.wait_ge(att_consts, 6)
            with me.loop(NPAIR, 10) as i:
                def soft(n):
                    hd, u = divmod(n, 5)
                    c = 80 if u == 0 else P * u
                    o = sp[:, hd, SPO[u]:SPO[u] + c]
                    dve.wait_ge(l_ready, i * 10 + (n + 1))
                    me.step(STT(o, pb[:, u, 0:c], 0.0, al[:, n % 2, 0:c], ALU.max, ALU.add))
                    me.settle()
                    d = sp[:, hd, 64:80] if u == 0 else o[:, 0:P]
                    TT(d, d, vis[:, 0:16] if u == 0 else vis[:, :], ALU.mult).then_inc(sp_ready, 1)

                def hide(n):
                    hd, u = divmod(n, 5)
                    w = w_att[:, n % 2, 64:80] if u == 0 else w_att[:, n % 2, 0:P]
                    dve.wait_ge(w_ready, i * 10 + (n + 1))
                    STT(w, w, 1.0, vis[:, 0:16] if u == 0 else vis[:, :], ALU.min, ALU.mult).then_inc(wm_ready, 1)

                def outputs_low(hd):
                    ps = slice(64 * hd, 64 * hd + 64)
                    dve.wait_ge(o_hi, i * 4 + (2 * hd + 2))
                    for c0, c1, o in [(0, 512, pb[ps, 5 + hd, :]), (512, L, pb[ps, 7, 0:16])]:
                        TT(hl[ps, bass.ds(i + 4, 1), c0:c1].squeeze(1), o,
                           hh[ps, bass.ds(i + 4, 1), c0:c1].squeeze(1).bitcast(F32), ALU.subtract).then_inc(o_evac, 1)

                for n in range(10):
                    soft(n)
                    if n >= 1:
                        hide(n - 1)
                    if n == 7:
                        outputs_low(0)
                hide(9)
                outputs_low(1)
            dve.wait_ge(o_evac, 16 + FREE)
            dve.sem_inc(mix_ready, 4)
            for m in range(4):
                dve.wait_ge(gate_ready, m + 1)
                TT(uqk[:, m, :], uqk[:, m, :], tmp[:, m % 2, :], ALU.mult).then_inc(glu_out, 1)
                dve.wait_ge(glu_out, m + 1)
                dve.sem_inc(tmp_free, 1)
            for m in range(4):
                dve.wait_ge(mix_hi, m + 1)
                TT(hl[:, m, 0:L], uqk[:, m, :], hh[:, m, 0:L].bitcast(F32), ALU.subtract).then_inc(mix_ready, 1)
            used[0] += 4

            def residual(name, scale, add):
                _, slots, _, per = STAGES[name]
                turn = 2 * per
                if add:
                    step(dve.memset(total[:, :], 0.0))
                with me.loop(slots // 2, 0) as i:
                    for t in range(turn):
                        _, _, t0, _ = STAGES[name]
                        hm = h[:, bass.ds(i * turn + t, 1), :].squeeze(1)
                        wait_tile(name, i, t)
                        STT(hm, hm, scale, tmp[:, (t0 + t) % 2, :], ALU.mult, ALU.add).then_inc(tmp_free, 1)
                        if add:
                            dve.wait_ge(tmp_free, i * turn + (used[0] + t + 3))
                            if True:
                                dve.wait_ge(summed, i * turn + (sums[0] + t) + FREE)
                            TT(total[:, :], total[:, :], hm, ALU.add).then_inc(summed, 1)
                used[0] += slots * per
                if add:
                    sums[0] += slots * per

            sums = [0]

            def inv_sqrt(guess, x_, t, o, n):
                dve.wait_ge(guessed, n)
                step(TT(t, guess, guess, ALU.mult))
                step(TT(t, t, x_, ALU.mult))
                step(TS(t, t, -0.5, 1.5, ALU.mult, ALU.add))
                step(TT(o, guess, t, ALU.mult))

            def layer_norm(n, last=False):
                layer, which = divmod(n, 2)
                dve.wait_ge(ln_mean, n + 1)
                for m in range(KC):
                    TT(halves(h[:, m, :]), halves(h[:, m, :]), pb[:, 4:6, 0:LH], ALU.subtract).then_inc(centred, 1)
                dve.wait_ge(sq_summed, 8 * n + 8)
                TS(halves(total[:, :]), pb[:, 6:8, 0:LH], LN_EPS, None, ALU.add).then_inc(var_out, 1)
                dve.wait_ge(var_out, n + 1)
                inv_sqrt(tmq[:, 0, :], total[:, :], tmq[:, 1, :], total[:, :], n + 1 + (8 if n >= 2 else 0))
                for m in range(KC + 1):
                    if m < KC:
                        TT(h[:, m, :], h[:, m, :], total[:, :], ALU.mult).then_inc(scaled, 1)
                    if m >= 1 and not last:
                        dve.wait_ge(ln_out, 8 * n + m)
                        dve.wait_ge(ln_hi, 8 * n + m)
                        TT(hl[:, m - 1, 0:L], h[:, m - 1, :], hh[:, m - 1, 0:L].bitcast(F32),
                           ALU.subtract).then_inc(ready, 1)

            def hidden(name, k0):
                _, slots, t0, per = STAGES[name]
                turn = 2 * per
                with me.loop(slots // 2, turn) as i:
                    for t in range(turn):
                        par = (t0 + t) % 2
                        a, r = tmq[:, par, :], tmp[:, par, :]
                        m = bass.ds(i * turn + t, 1)
                        wait_tile(name, i, t)
                        me.step(TT(a, r, r, ALU.mult))
                        TT(hidh[:, m, :].squeeze(1), r, r, ALU.mult).then_inc(tmp_free, 1)
                        me.settle()
                        dve.wait_ge(tmp_free, i * turn + (used[0] + t + 3))
                        TT(hidl[:, m, :].squeeze(1), a, hidh[:, m, :].squeeze(1).bitcast(F32),
                           ALU.subtract).then_inc(hid_ready, 1)
                used[0] += slots * per

            def mlp(layer):
                hidden(f"up{layer}0", 0)
                residual(f"down{layer}0", ALPHA, False)
                hidden(f"up{layer}1", 16)
                residual(f"down{layer}1", 1.0, True)

            residual("out_ab", ALPHA, True)
            layer_norm(0)
            mlp(0)
            layer_norm(1)

            dve.wait_ge(tile_done, STAGES["i"][2])
            me.step(dve.memset(keep[:, :], 1.0))
            me.step(dve.memset(sct[:, :, :], 0.0))
            me.step(dve.memset(rms_w[:, :], 1.0 / P))
            me.step(dve.memset(same[:, :], 1.0))
            me.settle()
            step(dve.memset(keep[:, 0:1], 0.0))
            step(dve.memset(keep[:, 16:L].rearrange("p (c j) -> p c j", j=64)[:, :, 0:1], 0.0))
            dve.memset(same[0:64, 64:128], 0.0).then_inc(hmask, 1)
            _, slots, t0, per = STAGES["f"]
            with me.loop(slots // 2, 3 * 4) as i:
                for t in range(4):
                    n = i * 4 + t
                    par = (t0 + t) % 2
                    e = tmp[:, par, :]
                    dve.wait_ge(f_ln, n + 1)
                    dve.tensor_tensor_scan(bc[:, :], keep[:, :], lf[:, :], 0.0, ALU.mult, ALU.add).then_inc(f_b, 1)
                    step(TS(e, e, lbp[:, 7, bass.ds(n, 1)], lbp[:, 6, bass.ds(n, 1)], ALU.mult, ALU.add))
                    dve.wait_ge(f_exp, n * 2 + 2)
                    TT(kd[:, bass.ds(n, 1), :].squeeze(1), e, tmq[:, par, :], ALU.mult).then_inc(f_kd, 1)
                    step(dve.tensor_copy(elast[:, bass.ds(n, 1), :].squeeze(1), qd[:, bass.ds(n, 1), 15:L:64].squeeze(1)))
                    step(dve.tensor_copy(elz[:, bass.ds(n, 1), :].squeeze(1), qd[:, bass.ds(n, 1), 15:L - 64:64].squeeze(1)))
                    dve.wait_ge(f_kd, n + 1)
                    dve.sem_inc(tmp_free, 1)
            step(dve.memset(elz[:, :, 0:1], 0.0))
            used[0] += 8
            _, slots, t0, per = STAGES["q"]
            with me.loop(slots // 2, 4) as i:
                for t in range(4):
                    n = i * 4 + t
                    wait_tile("q", i, t)
                    qn = qd[:, bass.ds(n, 1), :].squeeze(1)
                    step(TT(qn, qn, tmp[:, (t0 + t) % 2, :], ALU.mult))
                    dve.sem_inc(tmp_free, 1)
                    dve.sem_inc(q_done, 1)
            used[0] += 8
            _, slots, t0, per = STAGES["g"]
            with me.loop(slots // 2, 4 * 2) as i:
                for t in range(4):
                    n = i * 4 + t
                    wait_tile("g", i, t)
                    dve.wait_ge(g_exp, n + 1)
                    step(TS(sg[:, :], tmq[:, 0, :], 1.0, None, ALU.add))
                    dve.sem_inc(g_done, 1)
                    step(dve.reciprocal(sg[:, :], sg[:, :]))
                    TT(gs[:, bass.ds(n, 1), :].squeeze(1), sg[:, :], tmp[:, (t0 + t) % 2, :], ALU.mult).then_inc(tmp_free, 1)
                    dve.wait_ge(tmp_free, n + (used[0] + 3))
            used[0] += 8
            mask = same[:, :].bitcast(I32)
            def mask_scores(i):
                dve.wait_ge(scored, i + 1 + FREE)
                me.step(dve.memset(lbp[:, 0, 0:1], 0.0))
                dve.copy_predicated(sct[0:16, 0, 0:16], mask[0:16, 0:16], pb[0:16, 5, 0:16]).then_inc(sct_ready, 1)
                dve.copy_predicated(sct[:, 1:5, :], mask.unsqueeze(1).broadcast_to([P, 4, P]),
                                    pb[:, 4, :].rearrange("p (a b) -> p a b", a=4)).then_inc(sct_ready, 1)
                dve.tensor_copy(d0[:, :, :], elz[:, bass.ds(i, 1), :].broadcast_to([P, P, 8])).then_inc(d_ready, 1)

            def states(i):
                dve.wait_ge(kv_done, i + 1)
                for o, c0, c1 in [(pb[:, 1, P:2 * P], 0, 1), (pb[:, 2, :], 1, 8), (pb[:, 3, 0:384], 2, 8)]:
                    nc_ = o.shape[1] // P
                    TT(d1[:, :, c0:c1:2].rearrange("p v c -> p c v"), o.rearrange("p (c v) -> p c v", c=nc_),
                       elast[:, bass.ds(i, 1), c0:c1:2].squeeze(1).unsqueeze(2).broadcast_to([P, nc_, P]),
                       ALU.mult).then_inc(d_ready, 1)
                dve.wait_ge(d_ready, i * 4 + 4)
                dve.tensor_tensor_scan(d1[:, :, :].rearrange("p v c -> p (v c)"), d0[:, :, :].rearrange("p v c -> p (v c)"),
                                       d1[:, :, :].rearrange("p v c -> p (v c)"), 0.0, ALU.mult, ALU.add).then_inc(states_ready, 1)

            def take_ms(i):
                dve.wait_ge(ms_done, i * 2 + 2)
                TS(sg[:, 16:L], pb[:, 0, :], RMS_EPS, None, ALU.add).then_inc(ms_out, 1)
                TS(sg[:, 0:16], pb[:, 7, 64:80], RMS_EPS, None, ALU.add).then_inc(ms_out, 1)

            def finish(i):
                dve.wait_ge(ms_out, i * 2 + 2 + FREE)
                inv_sqrt(tmq[:, 0, :], sg[:, :], tmq[:, 1, :], sg[:, :], i + 3)
                step(TT(sg[:, :], sg[:, :], total[:, :], ALU.mult))
                dve.wait_ge(mix_ready, i + 8)
                STT(bc[:, :], sg[:, :], cols_b[:, bass.ds(i + 72, 1)], gs[:, bass.ds(i, 1), :].squeeze(1),
                    ALU.mult, ALU.mult).then_inc(ho, 1)
                dve.wait_ge(mix_hi, i + 5)
                dve.wait_ge(ho, i + 1)
                TT(hl[:, bass.ds(i, 1), 0:L].squeeze(1), bc[:, :], hh[:, bass.ds(i, 1), 0:L].squeeze(1).bitcast(F32),
                   ALU.subtract).then_inc(mix_ready, 1)

            dve.wait_ge(consts, 8)
            mask_scores(0)
            states(0)
            with me.loop(7, 6) as i:
                mask_scores(i + 1)
                take_ms(i)
                states(i + 1)
                finish(i)
            take_ms(7)
            finish(7)
            residual("out_c", ALPHA, True)
            layer_norm(2)
            mlp(1)
            layer_norm(3, last=True)
            for t in range(4):
                dve.wait_ge(ot_done, t + 1)
                dve.tensor_copy(o_tok[:, t, :], pb[:, 2 * (t % 2):2 * (t % 2) + 2, :].rearrange("p a b -> p (a b)")).then_inc(ot_copied, 1)


_INS = ['x', 'meta', 'w_in_ab', 's5_lam_re', 's5_lam_im', 's5_log_dt', 's5_b_re', 's5_b_im', 's5_c_re', 's5_c_im',
        's5_d', 's5_w_glu', 's5_b_glu', 'w_out_ab', 'w_in_c', 'hgrn_gamma', 'hgrn_norm_g', 'w_out_c',
        'ln_mix_g', 'ln_mix_b', 'mlp_w_up', 'mlp_b_up', 'mlp_w_down', 'mlp_b_down', 'ln_mlp_g', 'ln_mlp_b']


def kernel(**inputs):
    import numpy as _np
    import concourse.bacc as _bacc
    from concourse import mybir as _mybir
    from concourse.bass_utils import run_bass_kernel_spmd as _run

    nc = _bacc.Bacc("TRN2", target_bir_lowering=False, num_devices=1)
    arrays, args = {}, []
    for name in _INS:
        a = _np.ascontiguousarray(inputs[name])
        arrays[f"in_{name}"] = a
        args.append(nc.dram_tensor(f"in_{name}", a.shape, _mybir.dt.from_np(a.dtype), kind="ExternalInput").ap())
    args.append(nc.dram_tensor("out_h", (1, SEQ, D), F32, kind="ExternalOutput").ap())
    trunk(nc, *args)
    r = _run(nc, [arrays], core_ids=[0])
    return r.results[0]["out_h"]
```

```python
from contextlib import ExitStack, contextmanager

import concourse.bass as bass
from concourse import mybir

ALU = mybir.AluOpType
ACT = mybir.ActivationFunctionType
F32 = mybir.dt.float32
F32R = mybir.dt.float32r
I32 = mybir.dt.int32

P = 128
D = 1024
KC = D // P
SEQ, NMETA = 512, 16
L = SEQ + NMETA
LH = L // 2
LPAD = 640
ALPHA = 4.0 ** 0.25
LN_EPS = 1e-5
RMS_EPS = 1e-6
SLOT = 2048
CH = 4
NCH = L // CH
NBLK = 5
NPAIR = 4
HGC = 9
GATE_MAX = 43.0
MAGIC = 12582912.0
TWO_PI = (6.28125, 0.0019350051879882812, 3.0199159819e-07)
INV_TWO_PI = 0.15915494309189535

STAGES = {}


def _plan():
    slot = tile = 0
    for name, slots, per in [
        ("uqk", 6, 2), ("v", 2, NBLK), ("glu", 1, 4), ("out_ab", 4, 2),
        ("up00", 8, 2), ("down00", 8, 1), ("up01", 8, 2), ("down01", 8, 1),
        ("i", 4, NBLK), ("f", 4, 2), ("g", 4, 2), ("q", 4, 2), ("out_c", 4, 2),
        ("up10", 8, 2), ("down10", 8, 1), ("up11", 8, 2), ("down11", 8, 1),
    ]:
        STAGES[name] = (slot, slots, tile, per)
        slot += slots
        tile += slots * per
    return slot


_plan()


def tmp_tiles(before):
    names = list(STAGES)
    return sum(STAGES[n][1] * STAGES[n][3] for n in names[:names.index(before)] if n not in ("uqk", "v", "i"))


FREE = 1
NROWS = 13


class Chain:

    def __init__(self, eng, sem):
        self.eng, self.sem, self.base, self.count, self.turn = eng, sem, 0, 0, 0

    def step(self, ins):
        ins.then_inc(self.sem, 1)
        self.count += 1

    def settle(self):
        self.eng.wait_ge(self.sem, self.turn + (self.base + self.count))

    @contextmanager
    def loop(self, turns, per):
        self.base, self.count = self.base + self.count, 0
        with self.eng.Fori(0, turns) as i:
            self.turn = i * per
            yield i
        assert self.count == per, (self.count, per)
        self.base, self.count, self.turn = self.base + turns * per, 0, 0


def trunk(nc, x, meta, w_in_ab, s5_lam_re, s5_lam_im, s5_log_dt, s5_b_re, s5_b_im, s5_c_re, s5_c_im,
          s5_d, s5_w_glu, s5_b_glu, w_out_ab, w_in_c, hgrn_gamma, hgrn_norm_g, w_out_c,
          ln_mix_g, ln_mix_b, mlp_w_up, mlp_b_up, mlp_w_down, mlp_b_down, ln_mlp_g, ln_mlp_b, out):
    with ExitStack() as ctx:
        def sb(name, shape, dt=F32, where=ctx):
            return where.enter_context(nc.sbuf_tensor(name, shape, dt))

        def sem(name):
            return ctx.enter_context(nc.semaphore(name))

        h = sb("h", [P, KC, L])
        mi = ExitStack()
        btt = sb("btt", [P, 2, 4, P], F32, mi)
        kt = sb("kt", [P, 2, 4, CH, 32], F32, mi)
        bt = sb("bt", [P, 2, 4, CH, 32], F32, mi)
        b0r = sb("b0r", [P, 2, 4, CH, 32], F32, mi)
        cm = sb("cm", [P, 2, 2, 4, 5, 32], F32, mi)
        ss = sb("ss", [P, 2, 2, 4, NCH + 1], F32, mi)
        mi.close()
        hh = sb("hh", [P, KC, LPAD], F32R)
        hl = sb("hl", [P, KC, LPAD], F32R)
        raw = sb("raw", [P, 2, SLOT])
        wh = sb("wh", [P, 2, SLOT], F32R)
        wl = sb("wl", [P, 2, SLOT], F32R)
        tmp = sb("tmp", [P, 2, L])
        tmq = sb("tmq", [P, 2, L])
        total = sb("total", [P, L])
        ident = sb("ident", [P, P])
        mean_w = sb("mean_w", [P, P])
        cols_a = sb("cols_a", [P, P])
        cols_b = sb("cols_b", [P, 112])
        uqk_scale = sb("uqk_scale", [P, 3])
        lbp = sb("lbp", [P, 8, 8])

        m0 = ExitStack()
        uqk = sb("uqk", [P, 12, L], F32, m0)
        v0 = sb("v0", [P, NBLK, 512], F32, m0)
        m0a = ExitStack()
        pw = sb("pw", [P, 2, 16, 5], F32, m0a)
        bb = sb("bb", [P, 2, 16, 16], F32, m0a)
        cn = sb("cn", [P, 2, 4, 2, 64], F32, m0a)
        co = sb("co", [P, 2, 16, 16], F32, m0a)
        lin_a = sb("lin_a", [P, P], F32, m0a)
        lin_b = sb("lin_b", [112, P], F32, m0a)
        ldt = sb("ldt", [112, 2], F32, m0a)
        pt = sb("pt", [P, 26, 16], F32, m0a)
        wb = sb("wb", [P, 2, 16, CH, 16], F32, m0a)
        wc = sb("wc", [P, 2, 16, 5, 16], F32, m0a)
        group = sb("group", [P, 2], F32, m0a)
        ew = sb("ew", [P, 5, 16], F32, m0a)
        m0x = ExitStack()
        x_tok = sb("x_tok", [P, 4, D], F32, m0x)
        meta_tok = sb("meta_tok", [NMETA, D], F32, m0x)
        m0x.close()
        er = sb("er", [P, 16, NCH], F32, m0a)
        ei = sb("ei", [P, 16, NCH], F32, m0a)
        vq = sb("vq", [P, 4, 4, NCH], F32, m0a)
        m0a.close()
        m0b = ExitStack()
        ntri = sb("ntri", [P, P], F32, m0b)
        nones = sb("nones", [P, P], F32, m0b)
        vis = sb("vis", [P, P], F32, m0b)
        qs = sb("qs", [P, L], F32, m0b)
        ks = sb("ks", [P, LPAD], F32, m0b)
        vs = sb("vs", [P, NBLK, P], F32, m0b)
        al = sb("al", [P, 2, 512], F32, m0b)
        sp = sb("sp", [P, 2, 512], F32, m0b)
        later = sb("later", [P, 2, 512], F32, m0b)
        w_att = sb("w_att", [P, 2, 512], F32, m0b)
        m0b.close()
        m0.close()
        def carve(src, at, shape):
            n = 1
            for k in shape:
                n *= k
            names = [f"a{k}" for k in range(len(shape))]
            return src[:, at:at + n].rearrange(f"p ({' '.join(names)}) -> p {' '.join(names)}", **dict(zip(names, shape)))
        ga, ge = tmq[:, 0, :], tmq[:, 1, :]
        uj = [w.rearrange("p (a c) -> p a c", a=4)
              for w in (tmp[:, 0, :], tmp[:, 1, :], total[:, :])]
        rt = [tmq[:, par, :].rearrange("p (a c) -> p a c", a=4) for par in range(2)]

        m1 = ExitStack()
        v1 = sb("v1", [P, NBLK, D], F32, m1)
        kd = sb("kd", [P, 8, L], F32, m1)
        qd = sb("qd", [P, 8, L], F32, m1)
        gs = sb("gs", [P, 8, L], F32, m1)
        elast = sb("elast", [P, 8, HGC], F32, m1)
        sg = sb("sg", [P, L], F32, m1)
        bc = sb("bc", [P, L], F32, m1)
        elz = sb("elz", [P, 8, 8], F32, m1)
        vh = sb("vh", [P, NBLK, P], F32, m1)
        kdt = sb("kdt", [P, NBLK, P], F32, m1)
        sct = sb("sct", [P, NBLK, P], F32, m1)
        d1 = sb("d1", [P, P, 8], F32, m1)
        same = sb("same", [P, P], F32, m1)
        rms_w = sb("rms_w", [P, P], F32, m1)
        m1f = ExitStack()
        keep = sb("keep", [P, L], F32, m1f)
        lf = sb("lf", [P, L], F32, m1f)
        m1f.close()
        d0 = sb("d0", [P, P, 8], F32, m1)
        m1.close()

        m2 = ExitStack()
        hidh = sb("hidh", [P, 16, L], F32R, m2)
        hidl = sb("hidl", [P, 16, L], F32R, m2)
        m2.close()
        m3 = ExitStack()
        o_tok = sb("o_tok", [P, 4, D], F32, m3)
        m3.close()

        pb = ctx.enter_context(nc.psum_tensor("pb", [P, 8, 512], F32))

        UQ = [512] + [max(P * (4 - u), 16) for u in range(1, 5)]
        UW = [32] + [L - UQ[u] for u in range(1, 5)]

        def own_block(w, u):
            if u == 0:
                return (w[:, 0:32].rearrange("p (a b) -> p a b", a=2),
                        vis[:, 0:16].unsqueeze(1).broadcast_to([P, 2, 16]))
            return (w[:, 0:112], vis[:, 16:P]) if u == 4 else (w[:, 0:P], vis[:, :])

        def dense(t):
            b = 2 * (t % 2)
            return pb[:, b:b + 2, 0:LH]

        def halves(ap):
            return ap.rearrange("p (a c) -> p a c", a=2)

        rows_in = sem("rows_in")
        bc_in = sem("bc_in")
        x_in = sem("x_in")
        x_in_2 = sem("x_in_2")
        w_in = [sem("w_in_even"), sem("w_in_odd")]
        w_hi = sem("w_hi")
        w_lo = sem("w_lo")
        tile_done = sem("tile_done")
        evac = sem("evac")
        tmp_free = sem("tmp_free")
        consts = sem("consts")
        att_consts = sem("att_consts")
        act_self = sem("act_self")
        dve_self = sem("dve_self")
        xt_done = sem("xt_done")
        xt_hi = sem("xt_hi")
        xt_res = sem("xt_res")
        ready = sem("ready")
        mix_hi = sem("mix_hi")
        mix_ready = sem("mix_ready")
        hid_ready = sem("hid_ready")
        summed = sem("summed")
        ln_mean = sem("ln_mean")
        centred = sem("centred")
        squared = sem("squared")
        sq_summed = sem("sq_summed")
        var_out = sem("var_out")
        ms_out = sem("ms_out")
        guessed = sem("guessed")
        scaled = sem("scaled")
        ln_hi = sem("ln_hi")
        ln_out = sem("ln_out")
        rows_set = sem("rows_set")
        rows_t = sem("rows_t")
        par_dve = sem("par_dve")
        par_act = sem("par_act")
        c_turned = sem("c_turned")
        wb_ready = sem("wb_ready")
        wc_ready = sem("wc_ready")
        zeroed = sem("zeroed")
        bt_ready = sem("bt_ready")
        uj_ready = sem("uj_ready")
        cm_ready = sem("cm_ready")
        bt_turned = sem("bt_turned")
        btt_copied = sem("btt_copied")
        added = sem("added")
        rotated = sem("rotated")
        kern_done = sem("kern_done")
        kt_copied = sem("kt_copied")
        ss_ready = sem("ss_ready")
        y_done = sem("y_done")
        s5_y = sem("s5_y")
        ge_in = sem("ge_in")
        ge_gate = sem("ge_gate")
        ge_step = sem("ge_step")
        y_ready = sem("y_ready")
        gate_ready = sem("gate_ready")
        glu_out = sem("glu_out")
        ks_staged = sem("ks_staged")
        vs_staged = sem("vs_staged")
        z_ready = sem("z_ready")
        l_ready = sem("l_ready")
        sp_ready = sem("sp_ready")
        later_ready = sem("later_ready")
        acc_ready = sem("acc_ready")
        w_ready = sem("w_ready")
        wm_ready = sem("wm_ready")
        pv_done = sem("pv_done")
        o_hi = sem("o_hi")
        o_evac = sem("o_evac")
        hmask = sem("hmask")
        f_ln = sem("f_ln")
        f_b = sem("f_b")
        f_exp = sem("f_exp")
        f_kd = sem("f_kd")
        q_done = sem("q_done")
        g_exp = sem("g_exp")
        g_done = sem("g_done")
        k_staged = sem("k_staged")
        v_staged = sem("v_staged")
        k_turned = sem("k_turned")
        scored = sem("scored")
        kv_done = sem("kv_done")
        o_done = sem("o_done")
        ms_done = sem("ms_done")
        kdt_ready = sem("kdt_ready")
        o_out = sem("o_out")
        sct_ready = sem("sct_ready")
        d_ready = sem("d_ready")
        states_ready = sem("states_ready")
        ho = sem("ho")
        ot_done = sem("ot_done")
        ot_copied = sem("ot_copied")
        out_sem = sem("out_sem")

        block = ctx.enter_context(nc.Block())

        halves_of = [slice(0, 64), slice(64, 128)]

        def decays(eng, q):
            eng.memset(rt[q % 2][:, :, 0:1], 0.0)
            return eng.tensor_copy(rt[q % 2][:, :, 1:NCH],
                                    pt[:, 18, 4 * q:4 * q + 4].unsqueeze(2).broadcast_to([P, 4, NCH - 1]))

        def blocks(eng, o, x_, n):
            return eng.tensor_tensor(o.rearrange("p a k (g c) -> p (a k) g c", g=2),
                                      x_.rearrange("p a k c -> p (a k) c").unsqueeze(2).broadcast_to([P, n, 2, 16]),
                                      group[:, :].unsqueeze(1).unsqueeze(3).broadcast_to([P, n, 2, 16]), ALU.mult)

        def b_blocks(eng, q):
            for ri in range(2):
                ins = blocks(eng, bt[:, ri], wb[:, ri, 4 * q:4 * q + 4], 4 * CH)
            ins.then_inc(bt_ready, 1)
            eng.wait_ge(bt_ready, q + 1)
            for ri in range(2):
                ins = eng.tensor_copy(b0r[:, ri], bt[:, ri, :, 0:1, :].broadcast_to([P, 4, CH, 32]))
            return ins

        def c_blocks(eng, q):
            for ri in range(2):
                ins = blocks(eng, cm[:, q % 2, ri], wc[:, ri, 4 * q:4 * q + 4], 4 * 5)
            return ins

        def squares(m):
            return (tmq if m % 4 < 2 else tmp)[:, m % 2, :]

        def gain_shift(n, m):
            layer, which = divmod(n, 2)
            g, b = 32 * which + 8 * layer + m, 32 * which + 16 + 8 * layer + m
            return cols_a[:, g:g + 1], cols_a[:, b:b + 1]

        def y_bank(q):
            return 4 if q == 3 else 6

        @block.sync
        def _(sp_):
            def load(i, c, src, kcs=KC):
                sp_.wait_ge(w_lo, i * 2 + (c - 1))
                sp_.dma_start(raw[:, c % 2, :].rearrange("p (k n) -> p k n", k=kcs), src).then_inc(w_in[c % 2], 16)

            def stream(name, w, cols, kcs, col0=0, skip=0):
                s0, slots, _, _ = STAGES[name]
                wv = w.rearrange("(k p) n -> p k n", p=P)
                with sp_.Fori(0, (slots - skip) // 2) as i:
                    for j in range(2):
                        load(i, s0 + skip + j, wv[:, :, bass.ds(i * (2 * cols) + (col0 + (skip + j) * cols), cols)], kcs)

            def first_slot(n):
                sp_.dma_start(raw[:, n, :].rearrange("p (k n) -> p k n", k=KC),
                              w_in_ab[0].rearrange("(k p) n -> p k n", p=P)[:, :, n * 256:(n + 1) * 256]).then_inc(w_in[n], 16)

            xv = x[0].rearrange("(t p) d -> p t d", p=P)
            sp_.dma_start(meta_tok[:, :], meta).then_inc(x_in, 16)
            sp_.dma_start(x_tok[:, :, 0:D // 2], xv[:, :, 0:D // 2]).then_inc(x_in, 16)
            first_slot(0)
            sp_.dma_start(x_tok[:, :, D // 2:D], xv[:, :, D // 2:D]).then_inc(x_in_2, 16)
            first_slot(1)
            stream("uqk", w_in_ab[0], 256, KC, skip=2)
            stream("v", w_in_ab[0], 256, KC, col0=1536)
            s0 = STAGES["glu"][0]
            load(0, s0, s5_w_glu[0].rearrange("(k p) n -> p k n", p=P), 4)
            stream("out_ab", w_out_ab[0], 256, KC)

            def mlp(layer):
                for half in range(2):
                    stream(f"up{layer}{half}", mlp_w_up[layer], 256, KC, col0=2048 * half)
                    stream(f"down{layer}{half}", mlp_w_down[layer][2048 * half:2048 * (half + 1), :], P, 16)

            mlp(0)
            stream("i", w_in_c[0], 256, KC, col0=2 * D)
            stream("f", w_in_c[0], 256, KC, col0=D)
            stream("g", w_in_c[0], 256, KC, col0=3 * D)
            stream("q", w_in_c[0], 256, KC, col0=0)
            stream("out_c", w_out_c[0], 256, KC)
            mlp(1)
            ov = out[0].rearrange("(t p) d -> p t d", p=P)
            for half in range(2):
                cols = slice(512 * half, 512 * (half + 1))
                for t in (0, 2):
                    sp_.wait_ge(ot_copied, 4 * half + t + 2)
                    sp_.dma_start(ov[:, t:t + 2, cols], o_tok[:, t:t + 2, cols]).then_inc(out_sem, 16)
            sp_.wait_ge(out_sem, 16 * 4)

        @block.gpsimd
        def _(pool):
            def low(s, par):
                pool.wait_ge(w_hi, s + 1)
                pool.tensor_tensor(wl[:, par, :], raw[:, par, :], wh[:, par, :].bitcast(F32),
                                   ALU.subtract).then_inc(w_lo, 1)

            pool.memset(ident[:, :], 0.0).then_inc(consts, 1)
            pool.wait_ge(consts, 1)
            pool.affine_select(out=ident[:, :], in_=ident[:, :], compare_op=ALU.not_equal, fill=1.0,
                               base=0, pattern=[[-1, P]], channel_multiplier=1).then_inc(consts, 1)
            pool.memset(mean_w[:, :], 1.0 / D).then_inc(consts, 1)
            pool.memset(uqk_scale[:, 0:3:2], 1.0).then_inc(consts, 1)
            pool.memset(uqk_scale[:, 1:2], 64.0 ** -0.5).then_inc(consts, 1)
            pool.memset(hh[:, :, L:LPAD].bitcast(F32), 0.0).then_inc(consts, 1)
            pool.memset(hl[:, :, L:LPAD].bitcast(F32), 0.0).then_inc(consts, 1)
            low(0, 0)
            low(1, 1)

            def lows(name, pairs=None):
                s0, slots, _, _ = STAGES[name]
                with pool.Fori(0, pairs if pairs is not None else slots // 2) as i:
                    for j in range(2):
                        low(i * 2 + (s0 + 2 + j), (s0 + j) % 2)

            lows("uqk")
            lows("v")

            def stage_pair(i):
                if i:
                    pool.wait_ge(z_ready, i * 10)
                pool.tensor_copy(qs[:, :], uqk[:, i + 4, :]).then_inc(ks_staged, 1)
                pool.tensor_copy(ks[:, 0:L], uqk[:, i + 8, :]).then_inc(ks_staged, 1)
                if i:
                    pool.wait_ge(pv_done, i * 10 + FREE)
                pool.tensor_copy(vs[:, :, :], v0[:, :, i * P:(i + 1) * P]).then_inc(vs_staged, 1)

            pool.wait_ge(wb_ready, 1)
            pool.wait_ge(wc_ready, 1)
            for q in range(1, 4):
                pool.wait_ge(bt_turned, q)
                pool.wait_ge(kern_done, q)
                b_blocks(pool, q)
                if q >= 2:
                    pool.wait_ge(y_done, q - 1)
                    pool.wait_ge(ss_ready, q - 1)
                decays(pool, q)
                c_blocks(pool, q).then_inc(cm_ready, 1)
            pool.memset(ntri[:, :], -1.0).then_inc(att_consts, 1)
            pool.memset(nones[:, :], -1.0).then_inc(att_consts, 1)
            pool.memset(vis[:, :], 1.0).then_inc(att_consts, 1)
            pool.memset(ks[:, L:LPAD], 0.0).then_inc(att_consts, 1)
            pool.wait_ge(att_consts, 4)
            pool.affine_select(out=ntri[:, :], in_=ntri[:, :], compare_op=ALU.is_ge, fill=0.0,
                               base=0, pattern=[[-1, P]], channel_multiplier=1).then_inc(att_consts, 1)
            pool.affine_select(out=vis[:, :], in_=vis[:, :], compare_op=ALU.is_gt, fill=0.0,
                               base=0, pattern=[[1, P]], channel_multiplier=-1).then_inc(att_consts, 1)
            stage_pair(0)
            for i in range(NPAIR):
                if i:
                    stage_pair(i)
                y = uqk[:, i, :]
                pool.wait_ge(s5_y, 4 + FREE)
                pool.tensor_tensor(ga[:, :], y, y, ALU.mult).then_inc(ge_step, 1)
                pool.wait_ge(ge_step, i * 5 + 1)
                pool.tensor_scalar(ga[:, :], ga[:, :], 0.044715, 1.0, ALU.mult, ALU.add).then_inc(ge_step, 1)
                pool.wait_ge(ge_step, i * 5 + 2)
                pool.tensor_tensor(ga[:, :], ga[:, :], y, ALU.mult).then_inc(ge_step, 1)
                pool.wait_ge(ge_step, i * 5 + 3)
                pool.tensor_scalar(ga[:, :], ga[:, :], -GATE_MAX / 1.5957691216057308, None, ALU.max).then_inc(ge_in, 1)
                pool.wait_ge(ge_gate, i + 1)
                pool.tensor_tensor(y, y, ge[:, :], ALU.mult).then_inc(ge_step, 1)
                pool.wait_ge(ge_step, i * 5 + 4)
                yh = hh[:, i, 0:L]
                pool.tensor_copy(yh, y).then_inc(ge_step, 1)
                pool.wait_ge(ge_step, i * 5 + 5)
                pool.tensor_tensor(hl[:, i, 0:L], y, yh.bitcast(F32), ALU.subtract).then_inc(y_ready, 1)
            low(STAGES["glu"][0] + 2, 0)
            for name in ["out_ab", "up00", "down00", "up01", "down01", "i", "f", "g"]:
                lows(name)
            pool.wait_ge(hmask, 1)
            pool.affine_select(out=same[:, :], in_=same[:, :], compare_op=ALU.is_ge, fill=0.0,
                               base=0, pattern=[[1, P]], channel_multiplier=-1).then_inc(consts, 1)
            pool.wait_ge(tmp_free, tmp_tiles("q") + 2)
            pool.tensor_copy(tmq[:, 1, :], kd[:, 0, :]).then_inc(k_staged, 1)
            pool.tensor_copy(vh[:, :, :], v1[:, :, 0:P]).then_inc(v_staged, 1)
            lows("q")
            with pool.Fori(0, 7) as i:
                pool.wait_ge(scored, i + 1 + FREE)
                pool.tensor_copy(tmq[:, 1, :], kd[:, bass.ds(i + 1, 1), :]).then_inc(k_staged, 1)
                pool.wait_ge(o_done, i + 1 + FREE)
                pool.tensor_copy(vh[:, :, :], v1[:, :, bass.ds(i * P + P, P)]).then_inc(v_staged, 1)
            for name in ["out_c", "up10", "down10", "up11"]:
                lows(name)
            lows("down11", 3)

        @block.tensor
        def _(pe):
            pe.sem_inc(pv_done, FREE)
            pe.sem_inc(scored, FREE)
            pe.sem_inc(o_done, FREE)

            def prods(o, par, w0, w1, rh, rl, kc, first, last):
                lh, ll = wh[:, par, w0:w1], wl[:, par, w0:w1]
                for b in range(2):
                    pe.matmul(o[:, b, :], lh, rh[:, kc, b * LH:(b + 1) * LH], start=first, stop=False)
                for b in range(2):
                    pe.matmul(o[:, b, :], lh, rl[:, kc, b * LH:(b + 1) * LH], start=False, stop=False)
                for b in range(2):
                    mm = pe.matmul(o[:, b, :], ll, rh[:, kc, b * LH:(b + 1) * LH], start=False, stop=last)
                return mm

            def slot_tiles(s, par, t, t_par, per, kcs, cols, rh, rl, chunk_ready, order=None):
                pe.wait_ge(w_lo, s + 1)
                for j in range(per):
                    pe.wait_ge(evac, t + (j + 1))
                    for n, kc in enumerate(order or range(kcs)):
                        if j == 0 and chunk_ready:
                            pe.wait_ge(chunk_ready[0], chunk_ready[1] + n + 1)
                        w0 = kc * cols + j * P
                        mm = prods(dense(t_par + j), par, w0, w0 + P, rh, rl, kc, n == 0, n == kcs - 1)
                    mm.then_inc(tile_done, 1)

            def first_tiles(n, products):
                for kc in range(KC):
                    pe.wait_ge(ln_hi, 8 * n + kc + 1)
                    for j in range(2):
                        products(j, kc, True)
                for kc in range(KC):
                    pe.wait_ge(ready, 8 * (n + 1) + kc + 1)
                    for j in range(2):
                        mm = products(j, kc, False)
                        if kc == KC - 1:
                            mm.then_inc(tile_done, 1)

            def run_after(name, n):
                s0, slots, t0, per = STAGES[name]
                pe.wait_ge(w_lo, s0 + 1)
                pe.wait_ge(evac, t0 + 2)

                def products(j, kc, hi):
                    o, par, w = dense(t0 + j), s0 % 2, slice(kc * 256 + j * P, kc * 256 + (j + 1) * P)
                    for lhs, rhs, used_now in [(wh, hh, hi), (wl, hh, hi), (wh, hl, not hi)]:
                        if used_now:
                            for b in range(2):
                                mm = pe.matmul(o[:, b, :], lhs[:, par, w], rhs[:, kc, b * LH:(b + 1) * LH],
                                               start=kc == 0 and lhs is wh and hi, stop=kc == KC - 1 and not hi)
                    return mm

                first_tiles(n, products)
                slot_tiles(s0 + 1, (s0 + 1) % 2, t0 + per, t0 + per, per, KC, 256, hh, hl, None)
                run(name, KC, 256, hh, hl, None, first=1)

            def run(name, kcs, cols, rh, rl, chunk_ready, order=None, first=0):
                s0, slots, t0, per = STAGES[name]
                with pe.Fori(first, slots // 2) as i:
                    for j in range(2):
                        slot_tiles(i * 2 + (s0 + j), (s0 + j) % 2, i * (2 * per) + (t0 + j * per), t0 + j * per,
                                   per, kcs, cols, rh, rl, chunk_ready, order)

            def run_tok(name, starts, after=None):
                s0, slots, t0, per = STAGES[name]

                def tile(i, t, par, a):
                    pe.wait_ge(evac, i * (2 * per) + (t + 1))
                    o = pb[:, 2 * (t % 2), 0:256]
                    for kc in range(KC):
                        w = slice(kc * 256, (kc + 1) * 256)
                        pe.matmul(o, hh[:, kc, a:a + P], wh[:, par, w], start=kc == 0, stop=False)
                        pe.matmul(o, hh[:, kc, a:a + P], wl[:, par, w], start=False, stop=False)
                        mm = pe.matmul(o, hl[:, kc, a:a + P], wh[:, par, w], start=False, stop=kc == KC - 1)
                    mm.then_inc(tile_done, 1)

                def products(j, kc, hi):
                    a, par, w = starts[j], s0 % 2, slice(kc * 256, (kc + 1) * 256)
                    o = pb[:, 2 * ((t0 + j) % 2), 0:256]
                    if hi:
                        pe.matmul(o, hh[:, kc, a:a + P], wh[:, par, w], start=kc == 0, stop=False)
                        return pe.matmul(o, hh[:, kc, a:a + P], wl[:, par, w], start=False, stop=False)
                    return pe.matmul(o, hl[:, kc, a:a + P], wh[:, par, w], start=False, stop=kc == KC - 1)

                def pair_of_slots(i, done):
                    for j in range(2):
                        par = (s0 + j) % 2
                        pe.wait_ge(w_lo, i * 2 + (s0 + j + 1))
                        for k, a in enumerate(starts):
                            if j or k >= done:
                                tile(i, t0 + j * per + k, par, a)

                if after is not None:
                    pe.wait_ge(w_lo, s0 + 1)
                    pe.wait_ge(evac, t0 + 2)
                    first_tiles(after, products)
                    pair_of_slots(0, 2)
                with pe.Fori(0 if after is None else 1, slots // 2) as i:
                    pair_of_slots(i, 0)

            def keep_warm(count, bank):
                for _ in range(count):
                    pe.matmul(pb[:, bank, 0:P], ident[:, :], mean_w[:, :], start=True, stop=True)

            def layer_norm(n):
                keep_warm(12, 4)
                pe.wait_ge(summed, 8 * (n + 1) + FREE)
                for b in range(2):
                    mm = pe.matmul(pb[:, 4 + b, 0:LH], mean_w[:, :], total[:, b * LH:(b + 1) * LH],
                                   start=True, stop=True)
                mm.then_inc(ln_mean, 1)
                for m in range(KC):
                    pe.wait_ge(squared, 8 * n + m + 1)
                    for b in range(2):
                        mm = pe.matmul(pb[:, 6 + b, 0:LH], mean_w[:, :], squares(m)[:, b * LH:(b + 1) * LH],
                                       start=m == 0, stop=m == KC - 1)
                    mm.then_inc(sq_summed, 1)
                keep_warm(24, 4)

            def mlp(layer, n):
                for half in range(2):
                    if half == 0:
                        run_after(f"up{layer}0", n)
                    else:
                        run(f"up{layer}1", KC, 256, hh, hl, None)
                    run(f"down{layer}{half}", 16, P, hidh, hidl, (hid_ready, 16 * (2 * layer + half)))

            pe.wait_ge(consts, 2)
            pe.wait_ge(x_in, 32)
            for kc in range(KC):
                if kc == KC // 2:
                    pe.wait_ge(x_in_2, 16)
                if kc >= 2:
                    pe.wait_ge(xt_res, 2 * (kc - 1))
                b = 2 * (kc % 2)
                pe.transpose(pb[:, b, 0:NMETA], meta_tok[:, kc * P:(kc + 1) * P], ident[0:NMETA, 0:NMETA])
                for t in range(4):
                    o = pb[:, b, NMETA + t * P:NMETA + (t + 1) * P] if t < 3 else pb[:, b + 1, 0:P]
                    mm = pe.transpose(o, x_tok[:, t, kc * P:(kc + 1) * P], ident[:, :])
                mm.then_inc(xt_done, 1)
            pe.wait_ge(rows_in, 16 * NROWS)
            pe.wait_ge(rows_set, 2)
            pe.transpose(pb[:, 4, 0:P], lin_a[:, :], ident[:, :])
            pe.transpose(pb[:, 5, 0:112], lin_b[:, :], ident[0:112, 0:112]).then_inc(rows_t, 1)
            pe.wait_ge(xt_res, 16)
            pe.wait_ge(consts, 7)
            run("uqk", KC, 256, hh, hl, (ready, 0))
            pe.wait_ge(bc_in, 16 * 6)
            for ri in range(2):
                for q in range(4):
                    mm = pe.transpose(pb[:, 6 + ri, q * P:(q + 1) * P], cn[:, ri, q].rearrange("p d c -> p (d c)"),
                                      ident[:, :])
            mm.then_inc(c_turned, 1)
            run_tok("v", [b * P for b in range(NBLK)])

            pe.wait_ge(evac, STAGES["glu"][2] + 2)

            def turn_b(q):
                pe.wait_ge(bt_ready, q + 1)
                if q:
                    pe.wait_ge(kt_copied, q)
                for ri in range(2):
                    for p in range(4):
                        mm = pe.transpose(pb[:, 4 + ri, p * P:(p + 1) * P],
                                          bt[:, ri, p].rearrange("p a b -> p (a b)"), ident[:, :])
                mm.then_inc(bt_turned, 1)

            def outputs(q):
                pe.wait_ge(ss_ready, q + 1)
                pe.wait_ge(kt_copied, q + 1)
                if 0 < q < 3:
                    pe.wait_ge(s5_y, q + FREE)
                for p in range(4):
                    o = pb[:, y_bank(q) + p // 2, (p % 2) * NCH:(p % 2 + 1) * NCH]
                    pe.matmul(o, kt[:, q % 2, p].rearrange("p a b -> p (a b)"), uj[q % 3][:, p, :],
                              start=p % 2 == 0, stop=False, skip_group_check=True)
                    for ri in range(2):
                        mm = pe.matmul(o, cm[:, q % 2, ri, p, 1:5].rearrange("p a b -> p (a b)"),
                                       ss[:, q % 2, ri, p, 0:NCH],
                                       start=False, stop=(p % 2 == 1 and ri == 1), skip_group_check=True)
                mm.then_inc(y_done, 1)

            turn_b(0)
            for q in range(4):
                pe.wait_ge(btt_copied, q + 1)
                pe.wait_ge(uj_ready, q + 1)
                if q:
                    pe.wait_ge(rotated, q)
                for ri in range(2):
                    for p in range(4):
                        mm = pe.matmul(pb[:, 2 * ri + p // 2, (p % 2) * NCH:(p % 2 + 1) * NCH], btt[:, ri, p, :],
                                       uj[q % 3][:, p, :], start=p % 2 == 0, stop=p % 2 == 1, skip_group_check=True)
                mm.then_inc(added, 1)
                pe.wait_ge(cm_ready, q + 1)
                for p in range(4):
                    for ri in range(2):
                        mm = pe.matmul(pb[:, 4, p * P:(p + 1) * P], b0r[:, ri, p].rearrange("p a b -> p (a b)"),
                                       cm[:, q % 2, ri, p, 0:CH].rearrange("p a b -> p (a b)"),
                                       start=(p == 0 and ri == 0), stop=(p == 3 and ri == 1), skip_group_check=True)
                mm.then_inc(kern_done, 1)
                if q:
                    outputs(q - 1)
                if q < 3:
                    turn_b(q + 1)
            outputs(3)

            pe.wait_ge(att_consts, 6)
            pe.wait_ge(rotated, 4)
            pe.wait_ge(kt_copied, 4)

            def unit(n):
                return divmod(n, 5)

            def z(i, n):
                hd, u = unit(n)
                ps = slice(64 * hd, 64 * hd + 64)
                if n == 4:
                    pe.wait_ge(s5_y, 4 + FREE)
                if n >= 5:
                    pe.wait_ge(w_ready, i * 10 + (n - 4))
                b = 4 - u
                if u == 0:
                    pe.matmul(pb[:, 0, 0:16], ks[ps, 4 * P:5 * P], qs[ps, 512:L], start=True, stop=False,
                              skip_group_check=True)
                    mm = pe.matmul(pb[:, 0, 16:32], ks[ps, 0:P], qs[ps, 0:16], start=False, stop=True,
                                   skip_group_check=True)
                else:
                    mm = pe.matmul(pb[:, u, 0:UW[u]], ks[ps, b * P:(b + 1) * P], qs[ps, UQ[u]:L],
                                   start=True, stop=True)
                mm.then_inc(z_ready, 1)

            def acc(i, n):
                hd, u = unit(n)
                pe.wait_ge(sp_ready, i * 10 + (n + 1))
                pe.wait_ge(l_ready, i * 10 + (n + 1))
                if u:
                    pe.wait_ge(later_ready, i * 8 + (4 * hd + u))
                mm = pe.matmul(pb[:, u, 0:UW[u]], ntri[:, :], sp[:, n % 2, 0:UW[u]], start=False, stop=u == 0,
                               skip_group_check=True)
                if u:
                    a = UQ[u - 1] - 16
                    mm = pe.matmul(pb[:, u, UQ[u - 1] - UQ[u]:UW[u]], nones[:, :], later[:, (n - 1) % 2, a:512],
                                   start=False, stop=True, skip_group_check=True)
                mm.then_inc(acc_ready, 1)

            def pv(i, n):
                hd, u = unit(n)
                pe.wait_ge(wm_ready, i * 10 + (n + 1))
                if n == 0:
                    pe.wait_ge(vs_staged, i + 1)
                    pe.wait_ge(s5_y, 4 + FREE)
                if u == 0:
                    pe.wait_ge(o_evac, i * 4 + 2 * hd + FREE)
                    pe.matmul(pb[64 * hd:64 * hd + 64, 7, 0:16], vs[:, 0, 64 * hd:64 * hd + 64],
                              w_att[:, n % 2, 16:32], start=True, stop=True, skip_group_check=True)
                b, c = 4 - u, 16 if u == 0 else UW[u]
                mm = pe.matmul(pb[64 * hd:64 * hd + 64, 5 + hd, UQ[u] - 16:512], vs[:, b, 64 * hd:64 * hd + 64],
                               w_att[:, n % 2, 0:c], start=u == 0, stop=u == 4, skip_group_check=True)
                mm.then_inc(pv_done, 1)

            def pair(i, last):
                for n in range(10):
                    acc(i, n)
                    if n >= 2:
                        pv(i, n - 2)
                    if n < 7:
                        z(i, n + 3)
                    if n >= 8 and not last:
                        next_z(i, n - 8)
                if not last:
                    next_z(i, 2)
                pv(i, 8)
                pv(i, 9)

            def next_z(i, n):
                pe.wait_ge(ks_staged, i * 2 + 4)
                pe.wait_ge(w_ready, i * 10 + (6 + n))
                z(i + 1, n)

            pe.wait_ge(ks_staged, 2)
            z(0, 0)
            z(0, 1)
            z(0, 2)
            with pe.Fori(0, NPAIR - 1) as i:
                pair(i, False)
            pair(NPAIR - 1, True)

            s0, _, t0, per = STAGES["glu"]
            slot_tiles(s0, s0 % 2, t0, t0, per, 4, 512, hh, hl, (y_ready, 0))
            run("out_ab", KC, 256, hh, hl, (mix_ready, 0), order=[4, 5, 6, 7, 0, 1, 2, 3])
            layer_norm(0)
            mlp(0, 0)
            layer_norm(1)
            run_tok("i", [0] + [NMETA + t * P for t in range(4)], after=1)
            run("f", KC, 256, hh, hl, None)
            run("g", KC, 256, hh, hl, None)
            run("q", KC, 256, hh, hl, None)

            def keys(i):
                pe.wait_ge(k_staged, i + 1)
                pe.transpose(pb[0:16, 1, 0:P], tmq[:, 1, 0:16], ident[:, :])
                for t in range(4):
                    mm = pe.transpose(pb[:, 0, t * P:(t + 1) * P], tmq[:, 1, NMETA + t * P:NMETA + (t + 1) * P], ident[:, :])
                mm.then_inc(k_turned, 1)
                pe.matmul(pb[0:16, 5, 0:16], tmq[:, 1, 0:16], qd[:, bass.ds(i, 1), 0:16], start=True, stop=True)
                for t in range(4):
                    mm = pe.matmul(pb[:, 4, t * P:(t + 1) * P], tmq[:, 1, NMETA + t * P:NMETA + (t + 1) * P],
                                   qd[:, bass.ds(i, 1), NMETA + t * P:NMETA + (t + 1) * P],
                                   start=t == 0, stop=t == 3, skip_group_check=True)
                mm.then_inc(scored, 1)

            def chunk_sums(i):
                pe.wait_ge(kdt_ready, i * 2 + 2)
                pe.wait_ge(v_staged, i + 1)
                for c in range(8):
                    k = (c - 1) // 2
                    o = pb[:, 2 + (c + 1) % 2, k * P:(k + 1) * P] if c else pb[:, 1, P:2 * P]
                    if c == 0:
                        lt, rh = kdt[0:16, 0, :], vh[0:16, 0, :]
                    else:
                        t, r = 1 + (c - 1) // 2, 64 * ((c - 1) % 2)
                        lt, rh = kdt[r:r + 64, t, :], vh[r:r + 64, t, :]
                    mm = pe.matmul(o, lt, rh, start=c < 3, stop=c in (0, 6, 7), skip_group_check=True)
                mm.then_inc(kv_done, 1)

            def head_output(i):
                pe.wait_ge(sct_ready, i * 2 + 2)
                pe.wait_ge(ms_out, i * 2 + FREE)
                pe.matmul(pb[:, 7, 0:16], vh[0:16, 0, :], sct[0:16, 0, 0:16], start=True, stop=True)
                for t in range(4):
                    pe.matmul(pb[:, 6, t * P:(t + 1) * P], vh[:, 1 + t, :], sct[:, 1 + t, :],
                              start=t == 0, stop=False, skip_group_check=True)
                keep_warm(8, 0)
                pe.wait_ge(states_ready, i + 1)
                for c in range(1, HGC):
                    a = 64 * (c - 1)
                    mm = pe.matmul(pb[:, 6, a:a + 64], d1[:, :, c - 1], qd[:, bass.ds(i, 1), NMETA + a:NMETA + a + 64],
                                   start=False, stop=c == HGC - 1, skip_group_check=True)
                mm.then_inc(o_done, 1)

            def mean_squares(i):
                pe.wait_ge(o_out, i * 4 + 4)
                pe.matmul(pb[:, 7, 64:80], rms_w[:, :], tmq[:, 0, 0:16], start=True, stop=True).then_inc(ms_done, 1)
                pe.matmul(pb[:, 0, :], rms_w[:, :], tmq[:, 0, 16:L], start=True, stop=True).then_inc(ms_done, 1)

            pe.wait_ge(consts, 8)
            pe.wait_ge(q_done, 8)
            pe.wait_ge(evac, STAGES["out_c"][2] + 2)
            keys(0)
            chunk_sums(0)
            with pe.Fori(0, 7) as i:
                head_output(i)
                keys(i + 1)
                keep_warm(8, 3)
                pe.wait_ge(kdt_ready, i * 2 + 4)
                mean_squares(i)
                chunk_sums(i + 1)
            head_output(7)
            mean_squares(7)
            pe.wait_ge(ms_out, 16 + FREE)
            run("out_c", KC, 256, hh, hl, (mix_ready, 8))
            layer_norm(2)
            mlp(1, 2)
            layer_norm(3)
            for kc in range(KC):
                pe.wait_ge(ln_out, 24 + kc + 1)
                for t in range(4):
                    mm = pe.transpose(pb[:, 2 * t + kc // 4, (kc % 4) * P:(kc % 4 + 1) * P],
                                      h[:, kc, NMETA + t * P:NMETA + (t + 1) * P], ident[:, :])
                    if kc % 4 == 3:
                        mm.then_inc(ot_done, 1)

        @block.scalar
        def _(act):
            me = Chain(act, act_self)
            exp_ln = "natural_log_exp_and_others"
            act.preload_act_table_set(exp_ln)
            used = [0]

            def high(i, c):
                act.wait_ge(w_in[c % 2], i * 16 + 16 * (c // 2 + 1))
                act.activation(wh[:, c % 2, :], raw[:, c % 2, :], ACT.Copy).then_inc(w_hi, 1)

            def run(name, empty, split=True, pairs=None):
                s0, slots, t0, per = STAGES[name]
                with act.Fori(0, pairs if pairs is not None else slots // 2) as i:
                    for j in range(2):
                        body(name, empty, i, j, s0, t0, per, split)

            def body(name, empty, i, j, s0, t0, per, split):
                for k in range(per):
                    t = j * per + k
                    act.wait_ge(tile_done, i * (2 * per) + (t0 + t + 1))
                    empty(i, t, dense(t0 + t), (t0 + t) % 2).then_inc(evac, 1)
                if split:
                    high(i, s0 + j + 2)

            for k, src in enumerate([ln_mix_g, ln_mix_b, ln_mlp_g, ln_mlp_b]):
                act.dma_start(lin_a[16 * k:16 * k + 16, :], src.rearrange("l (k c) -> (l k) c", c=P)).then_inc(rows_in, 16)
            act.dma_start(lin_a[64:128, :], mlp_b_up.rearrange("l (k c) -> (l k) c", c=P)).then_inc(rows_in, 16)
            act.wait_ge(rows_set, 1)
            for r0, r1, src in [
                (0, 16, s5_lam_re[0].rearrange("(a s) c -> a (s c)", s=2)),
                (16, 32, s5_lam_im[0].rearrange("(a s) c -> a (s c)", s=2)),
                (32, 48, mlp_b_down.rearrange("l (k c) -> (l k) c", c=P)),
                (48, 52, s5_b_glu.rearrange("l (k c) -> (l k) c", c=P)),
                (52, 56, s5_d[0].rearrange("(k g) c -> k (g c)", k=4)),
                (56, 72, hgrn_gamma.rearrange("l (k c) -> (l k) c", c=P)),
                (72, 80, hgrn_norm_g.rearrange("l (k c) -> (l k) c", c=P)),
            ]:
                act.dma_start(lin_b[r0:r1, :], src).then_inc(rows_in, 16)
            act.dma_start(ldt[96:112, :], s5_log_dt[0].rearrange("(a s) -> a s", s=2)).then_inc(rows_in, 16)
            for ri, src in enumerate([s5_b_re, s5_b_im]):
                act.dma_start(bb[:, ri], src[0].rearrange("(a s) p h -> (s p) a h", s=2)).then_inc(bc_in, 16)
            for ri, src in enumerate([s5_c_re, s5_c_im]):
                for dup in range(2):
                    act.dma_start(cn[:, ri, :, dup, :],
                                  src[0].rearrange("(q g) h p -> (g h) q p", q=4)).then_inc(bc_in, 16)
            act.sem_inc(evac, 2)
            act.sem_inc(o_evac, FREE)

            for kc in range(KC):
                act.wait_ge(xt_res, 2 * (kc + 1))
                act.activation(hh[:, kc, 0:L], h[:, kc, :], ACT.Copy).then_inc(xt_hi, 1)
                if kc == 3:
                    high(0, 0)
            high(0, 1)

            act.wait_ge(par_dve, 1)
            act.activation(pt[:, 0, :], cols_b[:, 96:112], ACT.Exp).then_inc(par_act, 1)
            act.wait_ge(par_dve, 2)
            act.activation(pt[:, 3, :], pt[:, 1, :], ACT.Exp).then_inc(par_act, 1)
            act.activation(lbp[:, 3, :], lbp[:, 1, :], ACT.Exp).then_inc(par_act, 1)
            act.activation(lbp[:, 4, :], lbp[:, 2, :], ACT.Exp).then_inc(par_act, 1)
            act.wait_ge(par_dve, 3)
            act.activation(pt[:, 6, :], pt[:, 5, :], ACT.Sin).then_inc(par_act, 1)
            act.activation(pt[:, 7, :], pt[:, 5, :], ACT.Sin, scale=0.5).then_inc(par_act, 1)
            act.preload_act_table_set(exp_ln)

            def to_uqk(i, t, o, par):
                return act.activation(halves(uqk[:, bass.ds(i * 4 + t, 1), :].squeeze(1)), o, ACT.Identity,
                                      scale=uqk_scale[:, bass.ds(i, 1)])

            def to_tok(dst):
                def empty(i, t, o, par):
                    j, k = divmod(t, NBLK)
                    return act.activation(dst[:, k, bass.ds(i * 512 + j * 256, 256)], pb[:, 2 * par, 0:256], ACT.Copy)
                return empty

            act.wait_ge(consts, 7)
            run("uqk", to_uqk)

            def u_rows(q):
                for p in range(4):
                    ut = uqk[32 * p:32 * p + 32, q, :].rearrange("p (c j) -> p c j", j=CH)
                    for k in range(CH):
                        ins = act.activation(uj[q % 3][32 * k:32 * k + 32, p, :], ut[:, :, CH - 1 - k], ACT.Copy)
                ins.then_inc(uj_ready, 1)

            act.wait_ge(evac, STAGES["v"][2] + 2)
            u_rows(0)
            u_rows(1)
            run("v", to_tok(v0))

            act.wait_ge(zeroed, 1)
            for q in range(4):
                act.wait_ge(bt_turned, q + 1)
                if q:
                    act.wait_ge(added, q)
                for ri in range(2):
                    ins = act.activation(btt[:, ri].rearrange("p a b -> p (a b)"), pb[:, 4 + ri, :], ACT.Copy)
                ins.then_inc(btt_copied, 1)
                act.wait_ge(kern_done, q + 1)
                if q >= 2:
                    act.wait_ge(y_done, q - 1)
                for k in range(CH):
                    ins = act.activation(
                        kt[32 * k:32 * k + 32, q % 2, :, CH - 1 - k:CH, :],
                        pb[32 * k:32 * k + 32, 4, :].rearrange("p (a t c) -> p a t c", a=4, t=CH)[:, :, 0:k + 1, :],
                        ACT.Copy)
                ins.then_inc(kt_copied, 1)
                if q < 2:
                    if q == 1:
                        act.wait_ge(y_done, 1)
                    u_rows(q + 2)

            with me.loop(NPAIR, 22) as i:
                def pre(n):
                    hd, u = divmod(n, 5)
                    c = UW[u]
                    a = al[:, n % 2, 0:c]
                    act.wait_ge(z_ready, i * 10 + (n + 1))
                    if n >= 2:
                        act.wait_ge(sp_ready, i * 10 + (n - 1))
                    me.step(act.activation(a, pb[:, u, 0:c], ACT.Abs))
                    me.settle()
                    me.step(act.activation(a, a, ACT.Exp, scale=-1.0))
                    me.settle()
                    act.activation(a, a, ACT.Ln, bias=1.0).then_inc(l_ready, 1)

                def weigh(n):
                    hd, u = divmod(n, 5)
                    c = UW[u]
                    act.wait_ge(acc_ready, i * 10 + (n + 1))
                    if n >= 2:
                        act.wait_ge(pv_done, i * 10 + (n - 1 + FREE))
                    act.activation(w_att[:, n % 2, 0:c], pb[:, u, 0:c], ACT.Exp).then_inc(w_ready, 1)

                def outputs(hd):
                    ps = slice(64 * hd, 64 * hd + 64)
                    act.wait_ge(pv_done, i * 10 + (5 * hd + 5) + FREE)
                    act.activation(hh[ps, bass.ds(i + 4, 1), 16:L].squeeze(1), pb[ps, 5 + hd, :], ACT.Copy).then_inc(o_hi, 1)
                    act.activation(hh[ps, bass.ds(i + 4, 1), 0:16].squeeze(1), pb[ps, 7, 0:16], ACT.Copy).then_inc(o_hi, 1)

                for n in range(10):
                    pre(n)
                    if n >= 2:
                        weigh(n - 2)
                    if n == 7:
                        outputs(0)
                    if n == 4:
                        act.wait_ge(ge_in, i + 1)
                        me.step(act.activation(ge[:, :], ga[:, :], ACT.Exp, scale=-2.0 * 0.7978845608028654))
                        me.settle()
                        me.step(act.activation(ge[:, :], ge[:, :], ACT.Ln, bias=1.0))
                        me.settle()
                        act.activation(ge[:, :], ge[:, :], ACT.Exp, scale=-1.0).then_inc(ge_gate, 1)
                weigh(8)
                weigh(9)
                outputs(1)

            def into_tmp(name, func, **kw):
                first = used[0]
                _, slots, _, per = STAGES[name]
                used[0] += slots * per

                def empty(i, t, o, par):
                    act.wait_ge(tmp_free, i * (2 * per) + (first + t + 1))
                    more = {k: v(i, t) for k, v in kw.items()}
                    return act.activation(halves(tmp[:, par, :]), o, func, **more)
                return empty

            s0, _, t0, per = STAGES["glu"]
            used[0] += per
            for m in range(per):
                e = tmp[:, (t0 + m) % 2, :]
                act.wait_ge(evac, t0 + m + 3)
                me.step(act.activation(e, e, ACT.Exp, scale=-1.0))
                me.settle()
                me.step(act.activation(e, e, ACT.Ln, bias=1.0))
                me.settle()
                act.activation(e, e, ACT.Exp, scale=-1.0).then_inc(gate_ready, 1)
            high(0, s0 + 2)
            for m in range(4):
                act.wait_ge(glu_out, m + 1)
                act.activation(hh[:, m, 0:L], uqk[:, m, :], ACT.Copy).then_inc(mix_hi, 1)
            run("out_ab", into_tmp("out_ab", ACT.Copy))

            def guess_inv_sqrt(x_, o, ready_, n):
                act.wait_ge(ready_, n)
                me.step(act.activation(o, x_, ACT.Ln))
                me.settle()
                act.activation(o, o, ACT.Exp, scale=-0.5).then_inc(guessed, 1)

            def layer_norm(n, last=False):
                for m in range(KC):
                    act.wait_ge(centred, 8 * n + m + 1)
                    if m >= 4:
                        act.wait_ge(sq_summed, 8 * n + m - 3)
                    act.activation(squares(m), h[:, m, :], ACT.Square).then_inc(squared, 1)
                guess_inv_sqrt(total[:, :], tmq[:, 0, :], var_out, n + 1)
                for m in range(KC):
                    act.wait_ge(scaled, 8 * n + m + 1)
                    g, b = gain_shift(n, m)
                    if last:
                        act.activation(h[:, m, :], h[:, m, :], ACT.Identity, bias=b, scale=g).then_inc(ln_out, 1)
                    else:
                        act.activation(hh[:, m, 0:L], h[:, m, :], ACT.Identity, bias=b, scale=g).then_inc(ln_hi, 1)

            def mlp(layer, last=False):
                for half in range(2):
                    c0 = 64 + 32 * layer + 16 * half
                    run(f"up{layer}{half}", into_tmp(f"up{layer}{half}", ACT.Relu,
                                                     bias=lambda i, t: cols_a[:, bass.ds(i * 4 + (c0 + t), 1)]))
                    name = f"down{layer}{half}"
                    if half == 0:
                        run(name, into_tmp(name, ACT.Copy))
                    else:
                        empty = into_tmp(name, ACT.Identity,
                                         bias=lambda i, t: cols_b[:, bass.ds(i * 2 + (32 + 8 * layer + t), 1)])
                        if last:
                            run(name, empty, pairs=3)
                            s0, slots, t0, per = STAGES[name]
                            for j in range(2):
                                body(name, empty, 3, j, s0, t0, per, False)
                        else:
                            run(name, empty)

            layer_norm(0)
            mlp(0)
            layer_norm(1)
            run("i", to_tok(v1))

            s0, slots, t0, per = STAGES["f"]
            used[0] += slots * per
            with me.loop(slots // 2, 12) as i:
                for j in range(2):
                    for k in range(per):
                        t = j * per + k
                        n, par = i * 4 + t, (t0 + t) % 2
                        e = tmp[:, par, :]
                        act.wait_ge(evac, i * (2 * per) + (t0 + t + 3))
                        me.step(act.activation(e, e, ACT.Exp, scale=-1.0))
                        me.settle()
                        me.step(act.activation(e, e, ACT.Ln, bias=1.0))
                        me.settle()
                        me.step(act.activation(e, e, ACT.Exp, scale=-1.0))
                        me.settle()
                        act.activation(lf[:, :], e, ACT.Ln, bias=lbp[:, 5, bass.ds(n, 1)],
                                       scale=lbp[:, 6, bass.ds(n, 1)]).then_inc(f_ln, 1)
                        if k == 1:
                            high(i, s0 + j + 2)
                        act.wait_ge(f_b, n + 1)
                        act.activation(qd[:, bass.ds(n, 1), :].squeeze(1), bc[:, :], ACT.Exp).then_inc(f_exp, 1)
                        act.activation(tmq[:, par, :], bc[:, :], ACT.Exp, scale=-1.0).then_inc(f_exp, 1)
            gi = into_tmp("g", ACT.Copy)

            def gate(i, t, o, par):
                act.wait_ge(g_done, i * 4 + t + FREE)
                act.activation(halves(tmq[:, 0, :]), o, ACT.Exp, scale=-1.0).then_inc(g_exp, 1)
                return gi(i, t, o, par)
            run("g", gate)
            run("q", into_tmp("q", ACT.Copy))

            def take_k(i):
                act.wait_ge(k_turned, i + 1)
                act.activation(kdt[0:16, 0, :], pb[0:16, 1, 0:P], ACT.Copy).then_inc(kdt_ready, 1)
                act.activation(kdt[:, 1:5, :], pb[:, 0, :].rearrange("p (a b) -> p a b", a=4), ACT.Copy).then_inc(kdt_ready, 1)

            def take_o(i):
                act.wait_ge(o_done, i + 1 + FREE)
                act.activation(tmq[:, 0, 16:L], pb[:, 6, :], ACT.Square).then_inc(o_out, 1)
                act.activation(tmq[:, 0, 0:16], pb[:, 7, 0:16], ACT.Square).then_inc(o_out, 1)
                act.activation(total[:, 16:L], pb[:, 6, :], ACT.Copy).then_inc(o_out, 1)
                act.activation(total[:, 0:16], pb[:, 7, 0:16], ACT.Copy).then_inc(o_out, 1)

            def finish(i, at):
                guess_inv_sqrt(sg[:, :], tmq[:, 0, :], ms_out, i * 2 + 2 + FREE)
                act.wait_ge(ho, i + 1)
                act.activation(at, bc[:, :], ACT.Copy).then_inc(mix_hi, 1)

            take_k(0)
            with me.loop(7, 1) as i:
                take_o(i)
                take_k(i + 1)
                finish(i, hh[:, bass.ds(i, 1), 0:L].squeeze(1))
            take_o(7)
            finish(7, hh[:, 7, 0:L])
            run("out_c", into_tmp("out_c", ACT.Copy))
            layer_norm(2)
            mlp(1, last=True)
            layer_norm(3, last=True)

        @block.vector
        def _(dve):
            me = Chain(dve, dve_self)
            TT, TS, STT = dve.tensor_tensor, dve.tensor_scalar, dve.scalar_tensor_tensor
            used = [0]

            def wait_tile(name, i, t):
                _, _, t0, per = STAGES[name]
                dve.wait_ge(evac, i * (2 * per) + (t0 + t + 3))

            dve.memset(lin_b[:, :], 0.0).then_inc(rows_set, 1)
            dve.sem_inc(tmp_free, 2)
            for free in (s5_y, g_done, summed, ms_out):
                dve.sem_inc(free, FREE)

            dve.wait_ge(consts, 7)
            for kc in range(KC + 1):
                if kc < KC:
                    b = 2 * (kc % 2)
                    dve.wait_ge(xt_done, kc + 1)
                    dve.tensor_copy(h[:, kc, 0:400], pb[:, b, 0:400]).then_inc(xt_res, 1)
                    dve.tensor_copy(h[:, kc, 400:L], pb[:, b + 1, 0:P]).then_inc(xt_res, 1)
                if kc == KC - 1:
                    dve.wait_ge(rows_in, 16 * NROWS)
                    dve.wait_ge(rows_set, 1)
                    dve.tensor_copy(lin_b[96:112, :].rearrange("a (s c) -> a s c", s=2),
                                    ldt[96:112, :].unsqueeze(2).broadcast_to([16, 2, 64])).then_inc(rows_set, 1)
                if kc >= 1:
                    m = kc - 1
                    dve.wait_ge(xt_res, 2 * kc)
                    dve.wait_ge(xt_hi, kc)
                    TT(hl[:, m, 0:L], h[:, m, :], hh[:, m, 0:L].bitcast(F32), ALU.subtract).then_inc(ready, 1)

            dve.wait_ge(rows_t, 1)
            me.step(dve.tensor_copy(cols_a[:, :], pb[:, 4, 0:P]))
            dve.tensor_copy(cols_b[:, :], pb[:, 5, 0:112]).then_inc(par_dve, 1)

            def T(k):
                return pt[:, k, :]

            def step(ins):
                me.step(ins)
                me.settle()

            lr, li = cols_b[:, 0:16], cols_b[:, 16:32]
            dve.wait_ge(par_dve, 1)
            g0, g1 = cols_b[:, 56:64], cols_b[:, 64:72]
            step(TT(lbp[:, 0, :], g0, g1, ALU.max))
            step(TT(lbp[:, 1, :], g0, lbp[:, 0, :], ALU.subtract))
            step(TT(lbp[:, 2, :], g1, lbp[:, 0, :], ALU.subtract))
            dve.wait_ge(par_act, 1)
            TT(T(1), lr, T(0), ALU.mult).then_inc(par_dve, 1)
            step(TT(T(2), li, T(0), ALU.mult))
            step(TS(T(4), T(2), INV_TWO_PI, MAGIC, ALU.mult, ALU.add))
            step(TS(T(4), T(4), MAGIC, None, ALU.subtract))
            step(STT(T(5), T(4), -TWO_PI[0], T(2), ALU.mult, ALU.add))
            step(STT(T(5), T(4), -TWO_PI[1], T(5), ALU.mult, ALU.add))
            step(STT(T(5), T(4), -TWO_PI[2], T(5), ALU.mult, ALU.add))
            dve.wait_ge(par_dve, 2)
            TS(T(5), T(5), 3.1415925, -3.1415925, ALU.min, ALU.max).then_inc(par_dve, 1)
            dve.wait_ge(par_act, 4)
            step(TT(lbp[:, 0, :], lbp[:, 3, :], lbp[:, 4, :], ALU.add))
            step(dve.reciprocal(lbp[:, 0, :], lbp[:, 0, :]))
            step(TT(lbp[:, 1, :], lbp[:, 3, :], lbp[:, 0, :], ALU.mult))
            step(TT(lbp[:, 2, :], lbp[:, 4, :], lbp[:, 0, :], ALU.mult))
            step(TT(lbp[:, 5, :], lbp[:, 1, :], lbp[:, 2, :], ALU.add))
            step(TT(lbp[:, 5, :], lbp[:, 5, :], lbp[:, 1, :], ALU.subtract))
            step(TS(lbp[:, 6, :], lbp[:, 5, :], -1.0, 1.0, ALU.mult, ALU.add))
            step(TS(lbp[:, 7, :], lbp[:, 5, :], -1.0, None, ALU.add))
            dve.wait_ge(par_act, 6)
            step(TT(T(8), T(7), T(7), ALU.mult))
            step(TS(T(8), T(8), -2.0, 1.0, ALU.mult, ALU.add))
            step(TT(T(9), T(3), T(8), ALU.mult))
            step(TT(T(10), T(3), T(6), ALU.mult))
            step(TT(T(11), lr, lr, ALU.mult))
            step(TT(T(12), li, li, ALU.mult))
            step(TT(T(11), T(11), T(12), ALU.add))
            step(dve.reciprocal(T(11), T(11)))
            step(TS(T(12), T(9), -1.0, None, ALU.add))
            step(TT(T(13), T(12), lr, ALU.mult))
            step(TT(T(14), T(10), li, ALU.mult))
            step(TT(T(13), T(13), T(14), ALU.add))
            step(TT(T(13), T(13), T(11), ALU.mult))
            step(TT(T(15), T(10), lr, ALU.mult))
            step(TT(T(14), T(12), li, ALU.mult))
            step(TT(T(15), T(15), T(14), ALU.subtract))
            step(TT(T(15), T(15), T(11), ALU.mult))
            PR, PI = (lambda k: pw[:, 0, :, k]), (lambda k: pw[:, 1, :, k])
            step(dve.memset(PR(0), 1.0))
            step(dve.memset(PI(0), 0.0))
            step(dve.tensor_copy(PR(1), T(9)))
            step(dve.tensor_copy(PI(1), T(10)))
            for k, a, b in [(2, 1, 1), (3, 2, 1), (4, 2, 2)]:
                step(TT(T(16), PR(a), PR(b), ALU.mult))
                step(TT(T(17), PI(a), PI(b), ALU.mult))
                step(TT(PR(k), T(16), T(17), ALU.subtract))
                step(TT(T(16), PR(a), PI(b), ALU.mult))
                step(TT(T(17), PI(a), PR(b), ALU.mult))
                step(TT(PI(k), T(16), T(17), ALU.add))
            step(TT(T(18), T(3), T(3), ALU.mult))
            step(TT(T(18), T(18), T(18), ALU.mult))
            c, s = T(8), T(6)
            for k in (19, 21):
                step(TT(T(23), s, s, ALU.mult))
                step(TT(T(k + 1), s, c, ALU.mult))
                step(TS(T(k + 1), T(k + 1), 2.0, None, ALU.mult))
                step(TS(T(k), T(23), -2.0, 1.0, ALU.mult, ALU.add))
                c, s = T(k), T(k + 1)
            dve.wait_ge(bc_in, 16 * 6)
            fr, fi = (T(k).unsqueeze(2).broadcast_to([P, 16, 16]) for k in (13, 15))
            scratch = vq[:, :, :, :].rearrange("p v a c -> p (v a c)")
            u1, u2, u3, u4 = (carve(scratch, 256 * k, [16, 16]) for k in range(4))
            me.step(TT(u1, bb[:, 0], fr, ALU.mult))
            me.step(TT(u2, bb[:, 1], fi, ALU.mult))
            me.step(TT(u3, bb[:, 1], fr, ALU.mult))
            step(TT(u4, bb[:, 0], fi, ALU.mult))
            me.step(TT(bb[:, 0], u1, u2, ALU.subtract))
            step(TT(bb[:, 1], u3, u4, ALU.add))

            def powers_times(o, k1, srcr, srci, neg, done):
                t = carve(scratch, 0, [16, k1, 16])
                pr, pi = (pw[:, k, :, 0:k1].unsqueeze(3).broadcast_to([P, 16, k1, 16]) for k in range(2))
                xr, xi = (v.unsqueeze(2).broadcast_to([P, 16, k1, 16]) for v in (srcr, srci))
                step(TT(o[:, 0], pr, xr, ALU.mult))
                step(TT(t, pi, xi, ALU.mult))
                step(TT(o[:, 0], o[:, 0], t, ALU.subtract))
                step(TT(o[:, 1], pr, xi, ALU.mult))
                step(TT(t, pi, xr, ALU.mult))
                if neg:
                    line1 = o[:, 1].rearrange("p a b c -> p (a b c)")
                    STT(line1, line1, -1.0, t.rearrange("p a b c -> p (a b c)"), ALU.mult, ALU.subtract).then_inc(done, 1)
                else:
                    TT(o[:, 1], o[:, 1], t, ALU.add).then_inc(done, 1)
                dve.wait_ge(done, 1)

            for g, ps in enumerate(halves_of):
                me.step(dve.memset(group[ps, g:g + 1], 1.0))
                me.step(dve.memset(group[ps, 1 - g:2 - g], 0.0))
            me.settle()
            powers_times(wb, CH, bb[:, 0], bb[:, 1], False, wb_ready)
            step(dve.tensor_copy(ew[:, 0:2, :], pt[:, 21:23, :]))
            step(dve.memset(er[:, :, 0:1], 1.0))
            step(dve.memset(ei[:, :, 0:1], 0.0))
            n = 1
            while n < NCH:
                m = min(n, NCH - n)
                wr, wi = (ew[:, k, :].unsqueeze(2).broadcast_to([P, 16, m]) for k in (0, 1))
                a_, b_ = carve(scratch, 0, [16, m]), carve(scratch, 1024, [16, m])
                me.step(TT(a_, er[:, :, 0:m], wr, ALU.mult))
                step(TT(b_, ei[:, :, 0:m], wi, ALU.mult))
                step(TT(er[:, :, n:n + m], a_, b_, ALU.subtract))
                me.step(TT(a_, er[:, :, 0:m], wi, ALU.mult))
                step(TT(b_, ei[:, :, 0:m], wr, ALU.mult))
                step(TT(ei[:, :, n:n + m], a_, b_, ALU.add))
                n *= 2
                if n < NCH:
                    me.step(TT(ew[:, 2, :], ew[:, 0, :], ew[:, 0, :], ALU.mult))
                    me.step(TT(ew[:, 3, :], ew[:, 1, :], ew[:, 1, :], ALU.mult))
                    step(TT(ew[:, 4, :], ew[:, 0, :], ew[:, 1, :], ALU.mult))
                    me.step(TT(ew[:, 0, :], ew[:, 2, :], ew[:, 3, :], ALU.subtract))
                    step(TS(ew[:, 1, :], ew[:, 4, :], 2.0, None, ALU.mult))
            dve.wait_ge(c_turned, 1)
            for ri in range(2):
                for g, ps in enumerate(halves_of):
                    me.step(dve.tensor_copy(co[ps, ri], pb[ps, 6 + ri, :].rearrange("p (a g c) -> p a g c", a=16, g=2)[:, :, g, :]))
            me.settle()
            powers_times(wc, 5, co[:, 0], co[:, 1], True, wc_ready)
            decays(dve, 0)
            dve.wait_ge(tile_done, STAGES["glu"][2])
            b_blocks(dve, 0)
            dve.memset(kt[:, :, :, :, :].rearrange("p a b c d -> p (a b c d)"), 0.0).then_inc(zeroed, 1)
            c_blocks(dve, 0).then_inc(cm_ready, 1)
            me.step(dve.memset(ss[:, 0, :, :, 0:1], 0.0))
            step(dve.memset(ss[:, 1, :, :, 0:1], 0.0))

            def flat(v):
                return halves(v.rearrange("p a c -> p (a c)"))

            def line(v):
                return v.rearrange("p a c -> p (a c)")

            def outputs(q):
                dve.wait_ge(y_done, q + 1)
                for p in range(4):
                    ps = slice(32 * p, 32 * p + 32)
                    ut = uqk[ps, q, :].rearrange("p (c j) -> p c j", j=CH)
                    for t in range(CH):
                        ins = STT(ut[:, :, t], ut[:, :, t], cols_b[ps, 52 + q:53 + q],
                                  pb[32 * t:32 * t + 32, y_bank(q) + p // 2, (p % 2) * NCH:(p % 2 + 1) * NCH],
                                  ALU.mult, ALU.add)
                ins.then_inc(s5_y, 1)

            xr, xi = pb[:, 0:2, 0:LH], pb[:, 2:4, 0:LH]
            va, vb, vc, vd = (vq[:, k] for k in range(4))
            for q in range(4):
                eq, fq = er[:, 4 * q:4 * q + 4, :], ei[:, 4 * q:4 * q + 4, :]
                sr, si = (ss[:, q % 2, k, :, 1:NCH + 1] for k in range(2))
                dve.wait_ge(added, q + 1)
                me.step(TT(flat(va), flat(eq), xr, ALU.mult))
                me.step(TT(flat(vb), flat(fq), xi, ALU.mult))
                me.step(TT(flat(vc), flat(eq), xi, ALU.mult))
                TT(flat(vd), flat(fq), xr, ALU.mult).then_inc(rotated, 1)
                dve.wait_ge(rotated, q + 1)
                me.step(TT(va, va, vb, ALU.add))
                step(TT(vc, vc, vd, ALU.subtract))
                dve.wait_ge(cm_ready, q + 1)
                me.step(dve.tensor_tensor_scan(line(vb), line(rt[q % 2]), line(va), 0.0, ALU.mult, ALU.add))
                step(dve.tensor_tensor_scan(line(vd), line(rt[q % 2]), line(vc), 0.0, ALU.mult, ALU.add))
                if q >= 2:
                    dve.wait_ge(y_done, q - 1)
                me.step(TT(va, eq, vb, ALU.mult))
                step(TT(vc, fq, vd, ALU.mult))
                step(TT(sr, va, vc, ALU.subtract))
                me.step(TT(va, eq, vd, ALU.mult))
                step(TT(vc, fq, vb, ALU.mult))
                TT(si, va, vc, ALU.add).then_inc(ss_ready, 1)
                dve.wait_ge(ss_ready, q + 1)
                if q:
                    outputs(q - 1)
            outputs(3)

            dve.wait_ge(att_consts, 6)
            with me.loop(NPAIR, 16) as i:
                def soft(n):
                    hd, u = divmod(n, 5)
                    c = UW[u]
                    o = sp[:, n % 2, 0:c]
                    dve.wait_ge(l_ready, i * 10 + (n + 1))
                    if n >= 2:
                        dve.wait_ge(acc_ready, i * 10 + (n - 1))
                    me.step(STT(o, pb[:, u, 0:c], 0.0, al[:, n % 2, 0:c], ALU.max, ALU.add))
                    me.settle()
                    d, m = own_block(o, u)
                    TT(d, d, m, ALU.mult).then_inc(sp_ready, 1)

                def hide(n):
                    hd, u = divmod(n, 5)
                    w, m = own_block(w_att[:, n % 2, :], u)
                    dve.wait_ge(w_ready, i * 10 + (n + 1))
                    STT(w, w, 1.0, m, ALU.min, ALU.mult).then_inc(wm_ready, 1)

                def sum_later(n):
                    hd, u = divmod(n, 5)
                    if n >= 1:
                        dve.wait_ge(acc_ready, i * 10 + n)
                    o, a = later[:, n % 2, :], UQ[u] - 16
                    dve.wait_ge(sp_ready, i * 10 + (n + 1))
                    if u == 0:
                        dve.tensor_copy(o[:, a:512], sp[:, n % 2, 0:16]).then_inc(later_ready, 1)
                    else:
                        c = UQ[u - 1] - UQ[u]
                        me.step(dve.tensor_copy(o[:, a:a + c], sp[:, n % 2, 0:c]))
                        dve.wait_ge(later_ready, i * 8 + (4 * hd + u))
                        TT(o[:, a + c:512], sp[:, n % 2, c:UW[u]], later[:, (n - 1) % 2, a + c:512],
                           ALU.add).then_inc(later_ready, 1)

                def outputs_low(hd):
                    ps = slice(64 * hd, 64 * hd + 64)
                    dve.wait_ge(o_hi, i * 4 + (2 * hd + 2))
                    for c0, c1, o in [(16, L, pb[ps, 5 + hd, :]), (0, 16, pb[ps, 7, 0:16])]:
                        TT(hl[ps, bass.ds(i + 4, 1), c0:c1].squeeze(1), o,
                           hh[ps, bass.ds(i + 4, 1), c0:c1].squeeze(1).bitcast(F32), ALU.subtract).then_inc(o_evac, 1)

                for n in range(10):
                    soft(n)
                    if n % 5 < 4:
                        sum_later(n)
                    if n >= 2:
                        hide(n - 2)
                    if n == 7:
                        outputs_low(0)
                hide(8)
                hide(9)
                outputs_low(1)
            dve.wait_ge(o_evac, 16 + FREE)
            dve.sem_inc(mix_ready, 4)
            t0 = STAGES["glu"][2]
            for m in range(5):
                if m < 4:
                    dve.wait_ge(tile_done, t0 + m + 1)
                    TS(halves(tmp[:, (t0 + m) % 2, :]), dense(t0 + m), cols_b[:, 48 + m:49 + m], -GATE_MAX,
                       ALU.add, ALU.max).then_inc(evac, 1)
                if m >= 1:
                    n = m - 1
                    dve.wait_ge(gate_ready, n + 1)
                    TT(uqk[:, n, :], uqk[:, n, :], tmp[:, (t0 + n) % 2, :], ALU.mult).then_inc(glu_out, 1)
                    dve.wait_ge(glu_out, n + 1)
                    dve.sem_inc(tmp_free, 1)
            for m in range(4):
                dve.wait_ge(mix_hi, m + 1)
                TT(hl[:, m, 0:L], uqk[:, m, :], hh[:, m, 0:L].bitcast(F32), ALU.subtract).then_inc(mix_ready, 1)
            used[0] += 4

            def residual(name, scale, add):
                _, slots, _, per = STAGES[name]
                turn = 2 * per
                if add:
                    step(dve.memset(total[:, :], 0.0))
                with me.loop(slots // 2, 0) as i:
                    for t in range(turn):
                        _, _, t0, _ = STAGES[name]
                        hm = h[:, bass.ds(i * turn + t, 1), :].squeeze(1)
                        wait_tile(name, i, t)
                        STT(hm, hm, scale, tmp[:, (t0 + t) % 2, :], ALU.mult, ALU.add).then_inc(tmp_free, 1)
                        if add:
                            dve.wait_ge(tmp_free, i * turn + (used[0] + t + 3))
                            dve.wait_ge(summed, i * turn + (sums[0] + t) + FREE)
                            TT(total[:, :], total[:, :], hm, ALU.add).then_inc(summed, 1)
                used[0] += slots * per
                if add:
                    sums[0] += slots * per

            sums = [0]

            def inv_sqrt(guess, x_, t, o, n):
                dve.wait_ge(guessed, n)
                step(TT(t, guess, guess, ALU.mult))
                step(STT(t, t, -0.5, x_, ALU.mult, ALU.mult))
                step(STT(o, t, 1.5, guess, ALU.add, ALU.mult))

            def layer_norm(n, last=False):
                dve.wait_ge(ln_mean, n + 1)
                for m in range(KC):
                    TT(halves(h[:, m, :]), halves(h[:, m, :]), pb[:, 4:6, 0:LH], ALU.subtract).then_inc(centred, 1)
                dve.wait_ge(sq_summed, 8 * n + 8)
                TS(halves(total[:, :]), pb[:, 6:8, 0:LH], LN_EPS, None, ALU.add).then_inc(var_out, 1)
                dve.wait_ge(var_out, n + 1)
                inv_sqrt(tmq[:, 0, :], total[:, :], tmq[:, 1, :], total[:, :], n + 1 + (8 if n >= 2 else 0))
                for m in range(KC):
                    TT(h[:, m, :], h[:, m, :], total[:, :], ALU.mult).then_inc(scaled, 1)
                for m in range(0 if last else KC + 1):
                    if m < KC:
                        dve.wait_ge(ln_hi, 8 * n + m + 1)
                        g, b = gain_shift(n, m)
                        TS(h[:, m, :], h[:, m, :], g, b, ALU.mult, ALU.add).then_inc(ln_out, 1)
                    if m >= 1:
                        dve.wait_ge(ln_out, 8 * n + m)
                        TT(hl[:, m - 1, 0:L], h[:, m - 1, :], hh[:, m - 1, 0:L].bitcast(F32),
                           ALU.subtract).then_inc(ready, 1)

            def hidden(name):
                _, slots, t0, per = STAGES[name]
                turn = 2 * per
                with me.loop(slots // 2, turn) as i:
                    for t in range(turn):
                        par = (t0 + t) % 2
                        a, r = tmq[:, par, :], tmp[:, par, :]
                        m = bass.ds(i * turn + t, 1)
                        wait_tile(name, i, t)
                        me.step(TT(a, r, r, ALU.mult))
                        TT(hidh[:, m, :].squeeze(1), r, r, ALU.mult).then_inc(tmp_free, 1)
                        me.settle()
                        dve.wait_ge(tmp_free, i * turn + (used[0] + t + 3))
                        TT(hidl[:, m, :].squeeze(1), a, hidh[:, m, :].squeeze(1).bitcast(F32),
                           ALU.subtract).then_inc(hid_ready, 1)
                used[0] += slots * per

            def mlp(layer):
                hidden(f"up{layer}0")
                residual(f"down{layer}0", ALPHA, False)
                hidden(f"up{layer}1")
                residual(f"down{layer}1", 1.0, True)

            residual("out_ab", ALPHA, True)
            layer_norm(0)
            mlp(0)
            layer_norm(1)

            dve.wait_ge(tile_done, STAGES["i"][2])
            me.step(dve.memset(keep[:, :], 1.0))
            me.step(dve.memset(sct[:, :, :], 0.0))
            me.step(dve.memset(rms_w[:, :], 1.0 / P))
            me.step(dve.memset(same[:, :], 1.0))
            me.settle()
            step(dve.memset(keep[:, 0:1], 0.0))
            step(dve.memset(keep[:, 16:L].rearrange("p (c j) -> p c j", j=64)[:, :, 0:1], 0.0))
            dve.memset(same[0:64, 64:128], 0.0).then_inc(hmask, 1)
            _, slots, t0, per = STAGES["f"]

            def clamp(n):
                dve.wait_ge(tile_done, t0 + n + 1)
                TS(halves(tmp[:, (t0 + n) % 2, :]), dense(t0 + n), -GATE_MAX, None, ALU.max).then_inc(evac, 1)

            dve.wait_ge(evac, t0 + 2)
            clamp(0)
            for n in range(slots * per):
                par = (t0 + n) % 2
                e = tmp[:, par, :]
                dve.wait_ge(f_ln, n + 1)
                dve.tensor_tensor_scan(bc[:, :], keep[:, :], lf[:, :], 0.0, ALU.mult, ALU.add).then_inc(f_b, 1)
                me.step(TS(e, e, lbp[:, 7, n:n + 1], lbp[:, 6, n:n + 1], ALU.mult, ALU.add))
                if n + 1 < slots * per:
                    clamp(n + 1)
                dve.wait_ge(f_exp, n * 2 + 2)
                me.settle()
                TT(kd[:, n, :], e, tmq[:, par, :], ALU.mult).then_inc(f_kd, 1)
                me.step(dve.tensor_copy(elast[:, n, :], qd[:, n, 15:L:64]))
                me.step(dve.tensor_copy(elz[:, n, :], qd[:, n, 15:L - 64:64]))
                dve.wait_ge(f_kd, n + 1)
                dve.sem_inc(tmp_free, 1)
            me.settle()
            step(dve.memset(elz[:, :, 0:1], 0.0))
            used[0] += 8
            _, slots, t0, per = STAGES["g"]
            with me.loop(slots // 2, 4 * 2) as i:
                for t in range(4):
                    n = i * 4 + t
                    wait_tile("g", i, t)
                    dve.wait_ge(g_exp, n + 1)
                    step(TS(sg[:, :], tmq[:, 0, :], 1.0, None, ALU.add))
                    dve.sem_inc(g_done, 1)
                    step(dve.reciprocal(sg[:, :], sg[:, :]))
                    TT(gs[:, bass.ds(n, 1), :].squeeze(1), sg[:, :], tmp[:, (t0 + t) % 2, :], ALU.mult).then_inc(tmp_free, 1)
                    dve.wait_ge(tmp_free, n + (used[0] + 3))
            used[0] += 8
            _, slots, t0, per = STAGES["q"]
            with me.loop(slots // 2, 4) as i:
                for t in range(4):
                    n = i * 4 + t
                    wait_tile("q", i, t)
                    qn = qd[:, bass.ds(n, 1), :].squeeze(1)
                    step(TT(qn, qn, tmp[:, (t0 + t) % 2, :], ALU.mult))
                    dve.sem_inc(tmp_free, 1)
                    dve.sem_inc(q_done, 1)
            used[0] += 8
            mask = same[:, :].bitcast(I32)

            def mask_scores(i):
                dve.wait_ge(scored, i + 1 + FREE)
                me.step(dve.memset(lbp[:, 0, 0:1], 0.0))
                dve.copy_predicated(sct[0:16, 0, 0:16], mask[0:16, 0:16], pb[0:16, 5, 0:16]).then_inc(sct_ready, 1)
                dve.copy_predicated(sct[:, 1:5, :], mask.unsqueeze(1).broadcast_to([P, 4, P]),
                                    pb[:, 4, :].rearrange("p (a b) -> p a b", a=4)).then_inc(sct_ready, 1)
                dve.tensor_copy(d0[:, :, :], elz[:, bass.ds(i, 1), :].broadcast_to([P, P, 8])).then_inc(d_ready, 1)

            def states(i):
                dve.wait_ge(kv_done, i + 1)
                for o, c0, c1 in [(pb[:, 1, P:2 * P], 0, 1), (pb[:, 2, :], 1, 8), (pb[:, 3, 0:384], 2, 8)]:
                    nc_ = o.shape[1] // P
                    TT(d1[:, :, c0:c1:2].rearrange("p v c -> p c v"), o.rearrange("p (c v) -> p c v", c=nc_),
                       elast[:, bass.ds(i, 1), c0:c1:2].squeeze(1).unsqueeze(2).broadcast_to([P, nc_, P]),
                       ALU.mult).then_inc(d_ready, 1)
                dve.wait_ge(d_ready, i * 4 + 4)
                dve.tensor_tensor_scan(d1[:, :, :].rearrange("p v c -> p (v c)"), d0[:, :, :].rearrange("p v c -> p (v c)"),
                                       d1[:, :, :].rearrange("p v c -> p (v c)"), 0.0, ALU.mult, ALU.add).then_inc(states_ready, 1)

            def take_ms(i):
                dve.wait_ge(ms_done, i * 2 + 2)
                TS(sg[:, 16:L], pb[:, 0, :], RMS_EPS, None, ALU.add).then_inc(ms_out, 1)
                TS(sg[:, 0:16], pb[:, 7, 64:80], RMS_EPS, None, ALU.add).then_inc(ms_out, 1)

            def finish(i):
                dve.wait_ge(ms_out, i * 2 + 2 + FREE)
                inv_sqrt(tmq[:, 0, :], sg[:, :], tmp[:, 0, :], sg[:, :], i + 3)
                step(TT(sg[:, :], sg[:, :], total[:, :], ALU.mult))
                dve.wait_ge(mix_ready, i + 8)
                STT(bc[:, :], sg[:, :], cols_b[:, bass.ds(i + 72, 1)], gs[:, bass.ds(i, 1), :].squeeze(1),
                    ALU.mult, ALU.mult).then_inc(ho, 1)
                dve.wait_ge(mix_hi, i + 5)
                dve.wait_ge(ho, i + 1)
                TT(hl[:, bass.ds(i, 1), 0:L].squeeze(1), bc[:, :], hh[:, bass.ds(i, 1), 0:L].squeeze(1).bitcast(F32),
                   ALU.subtract).then_inc(mix_ready, 1)

            dve.wait_ge(consts, 8)
            mask_scores(0)
            states(0)
            with me.loop(7, 5) as i:
                mask_scores(i + 1)
                take_ms(i)
                states(i + 1)
                finish(i)
            take_ms(7)
            finish(7)
            residual("out_c", ALPHA, True)
            layer_norm(2)
            mlp(1)
            layer_norm(3, last=True)
            for half in range(2):
                for t in range(4):
                    dve.wait_ge(ot_done, 4 * half + t + 1)
                    dve.tensor_copy(o_tok[:, t, 512 * half:512 * (half + 1)], pb[:, 2 * t + half, :]).then_inc(ot_copied, 1)


_INS = ['x', 'meta', 'w_in_ab', 's5_lam_re', 's5_lam_im', 's5_log_dt', 's5_b_re', 's5_b_im', 's5_c_re', 's5_c_im',
        's5_d', 's5_w_glu', 's5_b_glu', 'w_out_ab', 'w_in_c', 'hgrn_gamma', 'hgrn_norm_g', 'w_out_c',
        'ln_mix_g', 'ln_mix_b', 'mlp_w_up', 'mlp_b_up', 'mlp_w_down', 'mlp_b_down', 'ln_mlp_g', 'ln_mlp_b']


def kernel(**inputs):
    import numpy as _np
    import concourse.bacc as _bacc
    from concourse import mybir as _mybir
    from concourse.bass_utils import run_bass_kernel_spmd as _run

    nc = _bacc.Bacc("TRN2", target_bir_lowering=False, num_devices=1)
    arrays, args = {}, []
    for name in _INS:
        a = _np.ascontiguousarray(inputs[name])
        arrays[f"in_{name}"] = a
        args.append(nc.dram_tensor(f"in_{name}", a.shape, _mybir.dt.from_np(a.dtype), kind="ExternalInput").ap())
    args.append(nc.dram_tensor("out_h", (1, SEQ, D), F32, kind="ExternalOutput").ap())
    trunk(nc, *args)
    r = _run(nc, [arrays], core_ids=[0])
    return r.results[0]["out_h"]
```
